# Optimizing a Trainium2 kernel written in Bass

```python
import jax, jax.numpy as jnp
from jax import lax
import numpy as np

D_MODEL = 1024
BATCH = 1
SEQ = 1024
DEPTH = 1

CTX_LEN = 256
GRID_W = 64
MLA_HEADS = 16
QK_NOPE = 64
QK_ROPE = 32
V_DIM = 64
Q_LORA = 256
KV_LORA = 128
ROPE_PAIRS = QK_ROPE // 4
ROPE_BASE = 10000.0
Q_BLOCK = 128
ATTN_SCALE = (QK_NOPE + QK_ROPE) ** -0.5
D_INNER = 2 * D_MODEL
SSM_HEAD_DIM = 64
SSM_HEADS = D_INNER // SSM_HEAD_DIM
SSM_GROUPS = 8
D_STATE = 128
D_CONV = 5
CHUNK = 128
CONV_DIM = D_INNER + 2 * SSM_GROUPS * D_STATE
D_FF = 4 * D_MODEL
N_MOD = 6
EPS = 1e-6
IN_SPLITS = (Q_LORA, KV_LORA, QK_ROPE, D_INNER, CONV_DIM, 2 * SSM_HEADS, D_MODEL, D_MODEL)
D_IN_PROJ = Q_LORA + KV_LORA + QK_ROPE + D_INNER + CONV_DIM + 2 * SSM_HEADS + 2 * D_MODEL

kernel_name = "hybrid_mla_ssd_dit_block"

def rmsnorm(u, g):
    uf = u.astype(jnp.float32)
    uf = uf * lax.rsqrt(jnp.mean(uf * uf, axis=-1, keepdims=True) + EPS)
    return uf.astype(u.dtype) * g

def modulate(h, shift, scale):
    return h * (1 + scale) + shift

def apply_axial_rope(u, cos, sin):
    us = u.reshape(u.shape[:-1] + (2, 2, ROPE_PAIRS))
    u1, u2 = us[..., 0, :], us[..., 1, :]
    out = jnp.stack([u1 * cos - u2 * sin, u2 * cos + u1 * sin], axis=-2)
    return out.reshape(u.shape)

def depthwise_conv(u, w, b):
    pad = (D_CONV - 1) // 2
    out = lax.conv_general_dilated(u, w[:, None, :], (1,), [(pad, pad)],
                                   dimension_numbers=('NWC', 'WIO', 'NWC'),
                                   feature_group_count=u.shape[-1])
    return out + b

def attend(q_nope, q_rope, k_nope, k_rope, v):
    b, n, h, _ = q_nope.shape
    nb = n // Q_BLOCK

    def to_blocks(t):
        return jnp.moveaxis(t.reshape((b, nb, Q_BLOCK) + t.shape[2:]), 1, 0)

    def one_block(qs):
        qn, qr = qs
        s = jnp.einsum('bqhd,bkhd->bhqk', qn, k_nope) + jnp.einsum('bqhr,bkr->bhqk', qr, k_rope)
        p = jax.nn.softmax(s.astype(jnp.float32) * ATTN_SCALE, axis=-1).astype(v.dtype)
        return jnp.einsum('bhqk,bkhd->bqhd', p, v)

    out = lax.map(one_block, (to_blocks(q_nope), to_blocks(q_rope)))
    return jnp.moveaxis(out, 0, 1).reshape(b, n, h * V_DIM)

def ssd_chunked(xs, dt, a, bm, cm, h0):
    f32 = jnp.float32
    b, n, h, p = xs.shape
    g, d_state = bm.shape[-2:]
    r = h // g
    nc = n // CHUNK
    x = xs.astype(f32).reshape(b, nc, CHUNK, g, r, p)
    dtc = dt.astype(f32).reshape(b, nc, CHUNK, g, r)
    a_cum = jnp.cumsum(dtc * a.astype(f32).reshape(g, r), axis=2)
    dtx = x * dtc[..., None]
    bc = bm.astype(f32).reshape(b, nc, CHUNK, g, d_state)
    cc = cm.astype(f32).reshape(b, nc, CHUNK, g, d_state)
    lower = jnp.tril(jnp.ones((CHUNK, CHUNK), bool))[:, :, None, None]
    seg = a_cum[:, :, :, None] - a_cum[:, :, None, :]
    decay = jnp.exp(jnp.where(lower, seg, -jnp.inf))
    cb = jnp.einsum('bcign,bcjgn->bcijg', cc, bc)
    y_diag = jnp.einsum('bcijgr,bcjgrp->bcigrp', cb[..., None] * decay, dtx)
    to_end = jnp.exp(a_cum[:, :, -1:] - a_cum)
    states = jnp.einsum('bcjgn,bcjgrp->bcgrpn', bc, dtx * to_end[..., None])
    chunk_decay = jnp.exp(a_cum[:, :, -1])

    def step(hs, inp):
        s, d = inp
        return hs * d[..., None, None] + s, hs

    h_last, h_before = lax.scan(step, h0.astype(f32),
                                (jnp.moveaxis(states, 1, 0), jnp.moveaxis(chunk_decay, 1, 0)))
    h_before = jnp.moveaxis(h_before, 0, 1)
    y_off = jnp.einsum('bcign,bcgrpn->bcigrp', cc, h_before) * jnp.exp(a_cum)[..., None]
    y = (y_diag + y_off).reshape(b, n, h, p)
    return y.astype(xs.dtype), h_last

def ssd_bidir(xs, dt, a, bm, cm, d_skip, h0_f, h0_b):
    y_f, h_f = ssd_chunked(xs, dt[:, :, 0], a[0], bm, cm, h0_f)
    flip = lambda t: jnp.flip(t, axis=1)
    y_b, h_b = ssd_chunked(flip(xs), flip(dt[:, :, 1]), a[1], flip(bm), flip(cm), h0_b)
    y = y_f + flip(y_b) + (d_skip[0] + d_skip[1])[:, None] * xs
    return y, h_f, h_b

def front(h, w_in, q_a_g, w_uq, kv_a_g, w_ukv, qk_q_g, qk_k_g, conv_w, conv_b, dt_bias):
    b, n, _ = h.shape
    proj = h @ w_in
    idx = np.cumsum(IN_SPLITS)[:-1].tolist()
    cq, ckv, k_rope, z, xbc, dt_raw, ga, gb = jnp.split(proj, idx, axis=-1)
    q = (rmsnorm(cq, q_a_g) @ w_uq).reshape(b, n, MLA_HEADS, QK_NOPE + QK_ROPE)
    kv = (rmsnorm(ckv, kv_a_g) @ w_ukv).reshape(b, n, MLA_HEADS, QK_NOPE + V_DIM)
    q_nope = rmsnorm(q[..., :QK_NOPE], qk_q_g[:QK_NOPE])
    q_rope = rmsnorm(q[..., QK_NOPE:], qk_q_g[QK_NOPE:])
    k_nope = rmsnorm(kv[..., :QK_NOPE], qk_k_g[:QK_NOPE])
    v = kv[..., QK_NOPE:]
    k_rope = rmsnorm(k_rope, qk_k_g[QK_NOPE:])
    xbc = jax.nn.silu(depthwise_conv(xbc, conv_w, conv_b))
    xs, bm, cm = jnp.split(xbc, [D_INNER, D_INNER + SSM_GROUPS * D_STATE], axis=-1)
    xs = xs.reshape(b, n, SSM_HEADS, SSM_HEAD_DIM)
    bm = bm.reshape(b, n, SSM_GROUPS, D_STATE)
    cm = cm.reshape(b, n, SSM_GROUPS, D_STATE)
    dt = jax.nn.softplus(dt_raw.reshape(b, n, 2, SSM_HEADS).astype(jnp.float32) + dt_bias)
    return q_nope, q_rope, k_nope, k_rope, v, z, xs, bm, cm, dt, ga, gb

def merge_branches(att, y_ssm, z, ga, gb, ssm_norm_g, w_proj_a, w_proj_b, w_out):
    b, n = att.shape[:2]
    u = y_ssm.reshape(b, n, D_INNER) * jax.nn.silu(z)
    u = rmsnorm(u.reshape(b, n, SSM_GROUPS, D_INNER // SSM_GROUPS),
                ssm_norm_g.reshape(SSM_GROUPS, D_INNER // SSM_GROUPS)).reshape(b, n, D_INNER)
    merged = jax.nn.sigmoid(ga) * (att @ w_proj_a) + jax.nn.sigmoid(gb) * (u @ w_proj_b)
    return merged @ w_out

def sq_relu_mlp(h, w1, w2):
    return jnp.square(jax.nn.relu(h @ w1)) @ w2

def setup_inputs(seed: int = 0) -> dict:
    key = jax.random.key(seed)
    ks = jax.random.split(key, 32)
    f32 = jnp.float32

    def dense(k, fan_in, shape, gain=1.0):
        return gain * fan_in ** -0.5 * jax.random.normal(k, shape, f32)

    def gain_init(k, shape):
        return 1.0 + 0.02 * jax.random.normal(k, shape, f32)

    dt0 = jnp.exp(jax.random.uniform(ks[20], (DEPTH, 2, SSM_HEADS), f32, np.log(1e-3), np.log(1e-1)))
    return {
        "x": jax.random.normal(ks[0], (BATCH, SEQ, D_MODEL), f32),
        "c": jax.random.normal(ks[1], (BATCH, D_MODEL), f32),
        "ctx": jax.random.normal(ks[2], (BATCH, CTX_LEN, D_MODEL), f32),
        "c_ctx": jax.random.normal(ks[3], (D_MODEL,), f32),
        "norm1_g": gain_init(ks[4], (DEPTH, D_MODEL)),
        "norm2_g": gain_init(ks[5], (DEPTH, D_MODEL)),
        "w_mod": dense(ks[6], D_MODEL, (DEPTH, D_MODEL, N_MOD * D_MODEL), 0.5),
        "b_mod": 0.01 * jax.random.normal(ks[7], (DEPTH, N_MOD * D_MODEL), f32),
        "w_in": dense(ks[8], D_MODEL, (DEPTH, D_MODEL, D_IN_PROJ)),
        "q_a_g": gain_init(ks[9], (DEPTH, Q_LORA)),
        "w_uq": dense(ks[10], Q_LORA, (DEPTH, Q_LORA, MLA_HEADS * (QK_NOPE + QK_ROPE))),
        "kv_a_g": gain_init(ks[11], (DEPTH, KV_LORA)),
        "w_ukv": dense(ks[12], KV_LORA, (DEPTH, KV_LORA, MLA_HEADS * (QK_NOPE + V_DIM))),
        "qk_q_g": gain_init(ks[13], (DEPTH, QK_NOPE + QK_ROPE)),
        "qk_k_g": gain_init(ks[14], (DEPTH, QK_NOPE + QK_ROPE)),
        "conv_w": dense(ks[15], D_CONV, (DEPTH, D_CONV, CONV_DIM)),
        "conv_b": 0.01 * jax.random.normal(ks[16], (DEPTH, CONV_DIM), f32),
        "dt_bias": dt0 + jnp.log(-jnp.expm1(-dt0)),
        "a_log": jnp.log(jax.random.uniform(ks[17], (DEPTH, 2, SSM_HEADS), f32, 1.0, 16.0)),
        "d_skip": gain_init(ks[18], (DEPTH, 2, SSM_HEADS)),
        "ssm_norm_g": gain_init(ks[19], (DEPTH, D_INNER)),
        "w_proj_a": dense(ks[21], MLA_HEADS * V_DIM, (DEPTH, MLA_HEADS * V_DIM, D_MODEL)),
        "w_proj_b": dense(ks[22], D_INNER, (DEPTH, D_INNER, D_MODEL)),
        "w_out": dense(ks[23], D_MODEL, (DEPTH, D_MODEL, D_MODEL)),
        "w_mlp1": dense(ks[24], D_MODEL, (DEPTH, D_MODEL, D_FF)),
        "w_mlp2": dense(ks[25], D_FF, (DEPTH, D_FF, D_MODEL)),
    }

def reference(x, c, ctx, c_ctx, norm1_g, norm2_g, w_mod, b_mod, w_in, q_a_g, w_uq, kv_a_g, w_ukv,
              qk_q_g, qk_k_g, conv_w, conv_b, dt_bias, a_log, d_skip, ssm_norm_g,
              w_proj_a, w_proj_b, w_out, w_mlp1, w_mlp2):
    f32 = jnp.float32
    b, n_lat, _ = x.shape
    rows = n_lat // GRID_W
    row = jnp.repeat(jnp.arange(rows), GRID_W)
    col = jnp.tile(jnp.arange(GRID_W), rows)
    freqs = ROPE_BASE ** (-jnp.arange(ROPE_PAIRS, dtype=f32) / ROPE_PAIRS)
    ang = jnp.stack([row, col], axis=-1).astype(f32)[..., None] * freqs
    cos, sin = jnp.cos(ang).astype(x.dtype), jnp.sin(ang).astype(x.dtype)

    c_act = jax.nn.silu(c)[:, None, :]
    cctx_act = jax.nn.silu(c_ctx)[None, None, :]
    h0 = jnp.zeros((b, SSM_GROUPS, SSM_HEADS // SSM_GROUPS, SSM_HEAD_DIM, D_STATE), f32)

    for l in range(DEPTH):
        mod_x = jnp.split(c_act @ w_mod[l] + b_mod[l], N_MOD, axis=-1)
        mod_c = jnp.split(cctx_act @ w_mod[l] + b_mod[l], N_MOD, axis=-1)
        layer_w = (w_in[l], q_a_g[l], w_uq[l], kv_a_g[l], w_ukv[l], qk_q_g[l], qk_k_g[l],
                   conv_w[l], conv_b[l], dt_bias[l])
        merge_w = (ssm_norm_g[l], w_proj_a[l], w_proj_b[l], w_out[l])
        a = -jnp.exp(a_log[l].astype(f32))

        hc = modulate(rmsnorm(ctx, norm1_g[l]), mod_c[0], mod_c[1])
        hx = modulate(rmsnorm(x, norm1_g[l]), mod_x[0], mod_x[1])
        qn_c, qr_c, kn_c, kr_c, v_c, z_c, xs_c, bm_c, cm_c, dt_c, ga_c, gb_c = front(hc, *layer_w)
        qn_x, qr_x, kn_x, kr_x, v_x, z_x, xs_x, bm_x, cm_x, dt_x, ga_x, gb_x = front(hx, *layer_w)
        qr_x = apply_axial_rope(qr_x, cos[:, None], sin[:, None])
        kr_x = apply_axial_rope(kr_x, cos, sin)

        y_c, h_f, h_b = ssd_bidir(xs_c, dt_c, a, bm_c, cm_c, d_skip[l], h0, h0)
        y_x, _, _ = ssd_bidir(xs_x, dt_x, a, bm_x, cm_x, d_skip[l], h_f, h_b)

        att_x = attend(qn_x, qr_x,
                       jnp.concatenate([kn_c, kn_x], axis=1),
                       jnp.concatenate([kr_c, kr_x], axis=1),
                       jnp.concatenate([v_c, v_x], axis=1))
        x = x + mod_x[2] * merge_branches(att_x, y_x, z_x, ga_x, gb_x, *merge_w)

        if l < DEPTH - 1:
            att_c = attend(qn_c, qr_c, kn_c, kr_c, v_c)
            ctx = ctx + mod_c[2] * merge_branches(att_c, y_c, z_c, ga_c, gb_c, *merge_w)
            hc2 = modulate(rmsnorm(ctx, norm2_g[l]), mod_c[3], mod_c[4])
            ctx = ctx + mod_c[5] * sq_relu_mlp(hc2, w_mlp1[l], w_mlp2[l])

        hx2 = modulate(rmsnorm(x, norm2_g[l]), mod_x[3], mod_x[4])
        x = x + mod_x[5] * sq_relu_mlp(hx2, w_mlp1[l], w_mlp2[l])
    return x


_drawn_inputs = setup_inputs


def setup_inputs(seed=0):
    import zlib

    import numpy as np

    out = dict(_drawn_inputs(seed))
    spreads = {}
    factors = {'ctx': 8.0,
     'c_ctx': 5.491,
     'norm1_g': 8.0,
     'norm2_g': 5.904,
     'b_mod': 3.532,
     'q_a_g': 8.0,
     'w_uq': 4.018,
     'kv_a_g': 8.0,
     'qk_q_g': 8.0,
     'qk_k_g': 8.0,
     'conv_b': 56.733,
     'd_skip': 64.0,
     'ssm_norm_g': 31.316}
    for name, (base, spread) in spreads.items():
        noise = np.random.default_rng([zlib.crc32(name.encode()), seed]).standard_normal(out[name].shape)
        drawn = base * np.exp(spread * noise) if base else spread * noise
        out[name] = __import__('jax').numpy.asarray(drawn.astype(out[name].dtype))
    for name, factor in factors.items():
        out[name] = (out[name] * factor).astype(out[name].dtype)
    return out
```

```python
from contextlib import ExitStack

import numpy as np

import concourse.bass as bass
from concourse import mybir

F32 = mybir.dt.float32
ALU = mybir.AluOpType
ACT = mybir.ActivationFunctionType
AX_X = mybir.AxisListType.X
PRIMED = 1

P = 128
D = 1024
KD = D // P
NLAT, NCTX = 1024, 256
NTOK = NLAT + NCTX
LT, CT = NLAT // P, NCTX // P
NT = LT + CT
HEADS, NOPE, ROPE, VD = 16, 64, 32, 64
QKD = NOPE + ROPE
PAIRS = HEADS // 2
QL, KVL = 256, 128
DI = 2 * D
SH, GROUPS, DS = 32, 8, 128
R = SH // GROUPS
HP = DI // SH
GC = DI // GROUPS
TAPS = 5
PAD = TAPS // 2
FF = 4 * D
EPS = 1e-6
SCALE = float(QKD) ** -0.5
COL_CQ, COL_KR = 0, QL + KVL
COL_Z = COL_KR + ROPE
COL_X = COL_Z + DI
COL_B = COL_X + DI
COL_C = COL_B + GROUPS * DS
COL_DT = COL_C + GROUPS * DS
COL_GA = COL_DT + 2 * SH
COL_GB = COL_GA + D
NC_SMALL = COL_Z
UP, LOW, SUP, SLOW = range(4)


def bcast(ap, *shape):
    return ap.to_broadcast([ap.shape[0], *shape])


class Count:

    def __init__(self, sem, step=1, primed=0):
        self.sem, self.step, self.base, self.n = sem, step, primed, 0

    def loop(self, i, per):
        self.entry, self.per = self.base + self.n * self.step, per
        self.base, self.n = self.entry + i * (per * self.step), 0

    def leave(self, turns):
        assert self.n == self.per, (self.sem, self.n, self.per)
        self.base, self.n = self.entry + turns * self.per * self.step, 0

    def add(self, k=1):
        self.n += k
        return self.value()

    def value(self, back=0):
        return self.base + (self.n - back) * self.step

    def raised(self, ins):
        ins.then_inc(self.sem, self.step)
        return self.add()


class Chain(Count):

    def __init__(self, eng, sem):
        super().__init__(sem)
        self.eng = eng

    def __call__(self, ins):
        self.eng.wait_ge(self.sem, self.raised(ins))


class Ctx:

    def __init__(self, nc, io):
        self.nc, self.io = nc, io
        self.tick = 0

    def sb(self, st, name, shape, dt=F32):
        return st.enter_context(self.nc.sbuf_tensor(name, shape, dt))

    def banks(self, st, name):
        return st.enter_context(self.nc.psum_tensor(name, [P, 8, 512], F32))

    def sem(self, st, name):
        return st.enter_context(self.nc.semaphore(name))


def modulation(k, keep):
    nc, io = k.nc, k.io
    with ExitStack() as st:
        cT = k.sb(st, "cT", [P, KD, 2])
        act_c = k.sb(st, "act_c", [P, KD, 2])
        act_b = k.sb(st, "act_b", [P, KD, P])
        wm = k.sb(st, "wm", [P, 4, KD, 512])
        bT = k.sb(st, "bT", [P, 48])
        brow = k.sb(st, "brow", [P, 2, D])
        n1 = k.sb(st, "n1", [P, KD])
        n2 = k.sb(st, "n2", [P, KD])
        gates = k.sb(st, "gates", [P, 2, D])
        modT = keep["modT"]
        ps = k.banks(st, "ps_mod")
        c_in = k.sem(st, "m_c_in")
        par_in = k.sem(st, "m_par_in")
        w_in = [k.sem(st, f"m_w_in{s}") for s in range(4)]
        w_done = k.sem(st, "m_w_done")
        acted = k.sem(st, "m_acted")
        spread = k.sem(st, "m_spread")
        gate_ev = k.sem(st, "m_gate_ev")
        gate_out = k.sem(st, "m_gate_out")
        chain = k.sem(st, "m_chain")
        blocks = [0, 1, 2, 3, 6, 7, 8, 9, 4, 5, 10, 11]
        block = st.enter_context(nc.Block())
        w = io["w_mod"][0].rearrange("(k p) n -> p k n", p=P)

        @block.sync
        def _(sp):
            sp.dma_start(cT[:], io["cvec"]).then_inc(c_in, 16)
            for n, b in enumerate(blocks):
                if n >= 4:
                    sp.wait_ge(w_done, n - 3)
                sp.dma_start(wm[:, n % 4], w[:, :, b * 512:(b + 1) * 512]).then_inc(w_in[n % 4], 16)
            sp.wait_ge(gate_ev, 4)
            sp.dma_start(io["gate_rows"], gates[:]).then_inc(gate_out, 16)
            sp.wait_ge(gate_out, 16)

        @block.gpsimd
        def _(pool):
            n = 0
            for dst, src in ((bT[:], io["b_modT"]), (n1[:], io["norm1"]), (n2[:], io["norm2"]),
                             (brow[:, 0], io["b_mod"][0, 2 * D:3 * D].partition_broadcast(P)),
                             (brow[:, 1], io["b_mod"][0, 5 * D:6 * D].partition_broadcast(P)),
                             (keep["ident"][:], io["ident"]), (keep["masks"][:], io["masks"])):
                pool.dma_start(dst, src).then_inc(par_in, 16)
                n += 16
            pool.wait_ge(par_in, n)

        @block.scalar
        def _(act):
            act.wait_ge(c_in, 16)
            act.activation(act_c[:], cT[:], ACT.Silu).then_inc(acted, 1)

        @block.tensor
        def _(pe):
            pe.wait_ge(acted, 1)
            for n, b in enumerate(blocks):
                pe.wait_ge(w_in[n % 4], 16 * (n // 4 + 1))
                if n < 8:
                    for c in range(4):
                        o = ps[:, 0, (4 * n + c) * 2:(4 * n + c) * 2 + 2]
                        for kk in range(KD):
                            mm = pe.matmul(o, wm[:, n % 4, kk, c * P:(c + 1) * P], act_c[:, kk],
                                           start=kk == 0, stop=kk == KD - 1)
                else:
                    if n == 8:
                        pe.wait_ge(spread, 1)
                    for kk in range(KD):
                        mm = pe.matmul(ps[:, n - 7], act_b[:, kk], wm[:, n % 4, kk], start=kk == 0, stop=kk == KD - 1)
                mm.then_inc(w_done, 1)

        @block.vector
        def _(dve):
            step = Chain(dve, chain)
            dve.wait_ge(acted, 1)
            dve.tensor_copy(act_b[:], bcast(act_c[:, :, 0:1], KD, P)).then_inc(spread, 1)
            dve.wait_ge(par_in, 16 * 7)
            dve.wait_ge(w_done, 8)
            raw = ps[:, 0, 0:64].rearrange("p (c s) -> p c s", s=2)
            for half, b0 in ((0, 0), (1, 24)):
                step(dve.tensor_tensor(modT[:, 16 * half:16 * half + 16], raw[:, 16 * half:16 * half + 16],
                                       bcast(bT[:, b0:b0 + 16].unsqueeze(2), 16, 2), ALU.add))
            for half, g in ((0, n1), (1, n2)):
                s = modT[:, 16 * half + 8:16 * half + 16]
                step(dve.tensor_scalar(s, s, 1.0, None, ALU.add))
                step(dve.tensor_tensor(s, s, bcast(g[:].unsqueeze(2), KD, 2), ALU.mult))
            for n in range(4):
                dve.wait_ge(w_done, n + 9)
                part = slice(512 * (n % 2), 512 * (n % 2) + 512)
                dve.tensor_tensor(gates[:, n // 2, part], ps[:, n + 1], brow[:, n // 2, part],
                                  ALU.add).then_inc(gate_ev, 1)


def norm_in(k, keep, hT):
    nc, io = k.nc, k.io
    modT, ident, eps = keep["modT"], keep["ident"], keep["eps"]
    with ExitStack() as st:
        xt = k.sb(st, "xt", [P, 4, D])
        xn = k.sb(st, "xn", [P, 2, D])
        junk = k.sb(st, "junk", [P, D])
        ss = k.sb(st, "ss", [P, 3, NT])
        ps = k.banks(st, "ps_norm")
        x_in = [k.sem(st, f"n_x_in{s}") for s in range(4)]
        rs = k.sem(st, "n_rs")
        xn_ok = k.sem(st, "n_xn")
        turned = k.sem(st, "n_turned")
        ev_a, ev_v = k.sem(st, "n_ev_a"), k.sem(st, "n_ev_v")
        eps_ok = k.sem(st, "n_eps")
        block = st.enter_context(nc.Block())

        @block.sync
        def _(sp):
            for t in range(NT):
                if t >= 4:
                    sp.wait_ge(xn_ok, t - 3)
                src = io["ctx"][0, t * P:(t + 1) * P] if t < CT else io["x"][0, (t - CT) * P:(t - CT + 1) * P]
                sp.dma_start(xt[:, t % 4], src).then_inc(x_in[t % 4], 16)

        @block.scalar
        def _(act):
            act.wait_ge(eps_ok, 1)

            def rstd(t):
                act.wait_ge(x_in[t % 4], 16 * (t // 4 + 1))
                act.activation(junk[:], xt[:, t % 4], ACT.Square, accum_out=ss[:, 0, t:t + 1]).then_inc(rs, 1)
                act.wait_ge(rs, 3 * t + 1)
                act.activation(ss[:, 1, t:t + 1], ss[:, 0, t:t + 1], ACT.Ln, bias=eps[:], scale=1.0 / D).then_inc(rs, 1)
                act.wait_ge(rs, 3 * t + 2)
                act.activation(ss[:, 2, t:t + 1], ss[:, 1, t:t + 1], ACT.Exp, scale=-0.5).then_inc(rs, 1)
            rstd(0)
            rstd(1)
            for t in range(NT):
                if t + 2 < NT:
                    rstd(t + 2)
                act.wait_ge(turned, 2 * t + 2)
                s = 1 if t < CT else 0
                for j in range(4):
                    ins = act.activation(hT[:, 4 + j, t * P:(t + 1) * P], ps[:, 2 * (t % 2) + 1, j * P:(j + 1) * P],
                                         ACT.Identity, bias=modT[:, 4 + j, s:s + 1], scale=modT[:, 12 + j, s:s + 1])
                ins.then_inc(ev_a, 1)

        def evac(dve, t):
            dve.wait_ge(turned, 2 * t + 1)
            s = 1 if t < CT else 0
            for j in range(4):
                ins = dve.tensor_scalar(hT[:, j, t * P:(t + 1) * P], ps[:, 2 * (t % 2), j * P:(j + 1) * P],
                                        modT[:, 8 + j, s:s + 1], modT[:, j, s:s + 1], ALU.mult, ALU.add)
            ins.then_inc(ev_v, 1)

        @block.vector
        def _(dve):
            dve.memset(eps[:], EPS).then_inc(eps_ok, 1)
            for t in range(NT):
                dve.wait_ge(rs, 3 * t + 3)
                if t >= 2:
                    dve.wait_ge(turned, 2 * t - 2)
                dve.tensor_scalar(xn[:, t % 2], xt[:, t % 4], ss[:, 2, t:t + 1], None, ALU.mult).then_inc(xn_ok, 1)
                if t >= 1:
                    evac(dve, t - 1)
            evac(dve, NT - 1)

        @block.tensor
        def _(pe):
            for t in range(NT):
                pe.wait_ge(xn_ok, t + 1)
                if t >= 2:
                    pe.wait_ge(ev_a, t - 1)
                    pe.wait_ge(ev_v, t - 1)
                for h in range(2):
                    for j in range(4):
                        ins = pe.transpose(ps[:, 2 * (t % 2) + h, j * P:(j + 1) * P],
                                           xn[:, t % 2, (4 * h + j) * P:(4 * h + j + 1) * P], ident[:])
                    ins.then_inc(turned, 1)


T_DT, T_WEND, T_EA, T_CD, T_DA = (i * NT * 2 * R for i in range(5))
T_SKIP = 5 * NT * 2 * R
T_ALL = T_SKIP + R


def step_chunk(d, s):
    if d == 0:
        return s
    return CT - 1 - s if s < CT else NT - 1 - (s - CT)


def ssd_tables(k, keep, hT, tab):
    nc, io = k.nc, k.io
    masks = keep["masks"]
    N = NT * 2 * SH
    with ExitStack() as st:
        wdt = k.sb(st, "wdt", [P, KD, P])
        bias = k.sb(st, "bias", [P, 2 * SH])
        alog = k.sb(st, "alog", [P, 2 * SH])
        skip = k.sb(st, "skip", [P, 2, SH])
        nega = k.sb(st, "nega", [P, 2 * SH])
        v, m, e, u, l, dd, dA = (k.sb(st, f"sp_{n}", [P, N]) for n in "vmeuldA")
        ones = k.sb(st, "ones", [P, P])
        ps = k.banks(st, "ps_dt")
        t_in, mm, chain, dve_ok, act_ok, dec = (k.sem(st, "t_" + n) for n in ("in", "mm", "chain", "dve", "act", "dec"))
        block = st.enter_context(nc.Block())

        def kind(col, d):
            g = tab[:, :, col:col + NT * 2 * R].rearrange("p g (c d r) -> p g c d r", d=2, r=R)[:, :, :, d]
            return g.rearrange("p g c r -> p c g r")

        def raw(t, d):
            return t[:].rearrange("p (c d h) -> p c d h", c=NT, d=2)[:, :, d]

        def raw4(t, d):
            return t[:].rearrange("p (c d g r) -> p c d g r", c=NT, d=2, r=R)[:, :, d]

        @block.sync
        def _(sp):
            sp.dma_start(wdt[:], io["w_in"][0].rearrange("(k p) n -> p k n", p=P)[:, :, COL_GA - P:COL_GA]).then_inc(t_in, 16)
            sp.dma_start(bias[:], io["dt_bias"][0].rearrange("d h -> (d h)").partition_broadcast(P)).then_inc(t_in, 16)
            sp.dma_start(alog[:], io["a_log"][0].rearrange("d h -> (d h)").partition_broadcast(P)).then_inc(t_in, 16)
            sp.dma_start(skip[:], io["d_skip"][0].partition_broadcast(P)).then_inc(t_in, 16)

        @block.tensor
        def _(pe):
            pe.wait_ge(t_in, 64)
            for t in range(NT):
                o = ps[:, t // 4, (t % 4) * P:(t % 4 + 1) * P]
                for kk in range(KD):
                    ins = pe.matmul(o, hT[:, kk, t * P:(t + 1) * P], wdt[:, kk], start=kk == 0, stop=kk == KD - 1)
            ins.then_inc(mm, 1)
            pe.wait_ge(dve_ok, 2)
            for b, (w, d) in enumerate(((SLOW, 0), (SUP, 1), (UP, 0), (LOW, 1), (None, 0), (None, 1))):
                pe.matmul(ps[:, 2 + b, 0:NT * SH], ones[:] if w is None else masks[:, w], raw(dA, d),
                          start=True, stop=True).then_inc(dec, 1)

        @block.scalar
        def _(act):
            act.wait_ge(t_in, 64)
            act.activation(nega[:], alog[:], ACT.Exp).then_inc(act_ok, 1)
            act.wait_ge(dve_ok, 1)
            act.activation(e[:], e[:], ACT.Exp).then_inc(act_ok, 1)
            act.wait_ge(act_ok, 2)
            act.activation(l[:], e[:], ACT.Ln, bias=1.0).then_inc(act_ok, 1)
            for b, (col, d) in enumerate(((T_WEND, 0), (T_WEND, 1), (T_EA, 0), (T_EA, 1))):
                act.wait_ge(dec, b + 1)
                act.activation(kind(col, d), ps[:, 2 + b, 0:NT * SH].rearrange("p (c g r) -> p c g r", c=NT, r=R),
                               ACT.Exp).then_inc(act_ok, 1)
            for d in range(2):
                act.wait_ge(dec, 5 + d)
                for s in range(NT):
                    c = step_chunk(d, s)
                    ins = act.activation(kind(T_CD, d)[:, s], ps[:, 6 + d, c * SH:(c + 1) * SH].rearrange("p (g r) -> p g r", r=R), ACT.Exp)
            ins.then_inc(act_ok, 1)

        @block.vector
        def _(dve):
            step = Chain(dve, chain)
            step(dve.memset(ones[:], 1.0))
            dve.wait_ge(mm, 1)
            for b, n in ((0, 4), (1, 4), (2, NT - 8)):
                step(dve.tensor_tensor(v[:, b * 256:b * 256 + n * 64].rearrange("p (c h) -> p c h", h=64),
                                       ps[:, b, 0:n * P].rearrange("p (c h) -> p c h", h=P)[:, :, P - 64:],
                                       bcast(bias[:].unsqueeze(1), n, 64), ALU.add))
            step(dve.tensor_scalar(m[:], v[:], 0.0, None, ALU.max))
            step(dve.tensor_scalar(e[:], v[:], -1.0, None, ALU.mult))
            dve.tensor_tensor(e[:], e[:], v[:], ALU.min).then_inc(dve_ok, 1)
            dve.wait_ge(act_ok, 3)
            step(dve.tensor_scalar(u[:], e[:], 1.0, -1.0, ALU.add, ALU.add))
            step(dve.tensor_scalar(dd[:], u[:], 0.0, None, ALU.is_equal))
            step(dve.tensor_tensor(u[:], u[:], dd[:], ALU.add))
            step(dve.tensor_tensor(l[:], l[:], dd[:], ALU.add))
            step(dve.tensor_tensor(l[:], l[:], e[:], ALU.mult))
            step(dve.reciprocal(u[:], u[:]))
            step(dve.tensor_tensor(l[:], l[:], u[:], ALU.mult))
            step(dve.tensor_tensor(m[:], l[:], m[:], ALU.add))
            step(dve.tensor_scalar(nega[:], nega[:], -1.0, None, ALU.mult))
            dve.tensor_tensor(dA[:].rearrange("p (c h) -> p c h", h=64), m[:].rearrange("p (c h) -> p c h", h=64),
                              bcast(nega[:].unsqueeze(1), NT, 64), ALU.mult).then_inc(dve_ok, 1)
            dve.wait_ge(dve_ok, 2)
            for d in range(2):
                dve.tensor_copy(kind(T_DT, d), raw4(m, d))
                dve.tensor_copy(kind(T_DA, d), raw4(dA, d))
            dve.tensor_tensor(tab[:, :, T_SKIP:T_ALL], skip[:, 0].rearrange("p (g r) -> p g r", r=R),
                              skip[:, 1].rearrange("p (g r) -> p g r", r=R), ALU.add)
            dve.wait_ge(act_ok, 7)
            for d in range(2):
                dve.tensor_tensor(kind(T_WEND, d), kind(T_WEND, d), raw4(m, d), ALU.mult)


XPAD = NCTX + PAD
CONVN = NCTX + PAD + NLAT
SEGS = ((0, 0, NCTX), (XPAD, NCTX, 512), (XPAD + 512, NCTX + 512, 512))
TURN_ORDER = [0, 1] + [c for s in range(2, 2 + LT // 2) for c in (s, NT - 1 + CT - s)]
STEPS = NT - 1
RING = 4 * 3 - 1 + LT // 2 + NT + 4


def tok_col(c):
    return c * P if c < CT else XPAD + (c - CT) * P


def ssd_groups(k, keep, hT, tab):
    nc, io = k.nc, k.io
    masks, ident, eps = keep["masks"], keep["ident"], keep["eps"]
    w = io["w_in"][0].rearrange("(k p) n -> p k n", p=P)
    with ExitStack() as st:
        sb = lambda n, s: k.sb(st, n, s)
        sem = lambda n: k.sem(st, "s_" + n)
        wx = sb("wx", [P, 4, KD, P])
        wz = sb("wz", [P, KD, GC])
        conv = sb("conv", [P, GROUPS, 4, TAPS + 1])
        gains = sb("gains", [P, GROUPS, 2])
        cg = sb("cg", [P, 4, TAPS + 1])
        tg = sb("tg", [P, T_ALL])
        sg = sb("sg", [P, 2])
        pre = sb("pre", [P, 2, CONVN + 2 * PAD])
        cv = sb("cv", [P, 2, CONVN])
        xb = sb("xb", [P, 4, CONVN])
        tk = sb("tk", [P, NT, GC + DS])
        u = sb("u", [P, LT, GC])
        H = sb("H", [P, STEPS, 2 * GC])
        xw = sb("xw", [P, 2, 2, GC])
        sr = sb("sr", [P, 2, 2, R * P])
        E = sb("E", [P, 2, R * P])
        cbm = sb("cbm", [P, 2, P])
        EC = sb("EC", [P, 2, 2, R * P])
        dtx = sb("dtx", [P, 2, 2, GC])
        t1 = sb("t1", [P, 2, 2, GC])
        xd = sb("xd", [P, GC])
        ss = sb("ss_u", [P, 3, LT])
        uo = sb("uo", [P, 2, 512])
        junk = sb("junk_u", [P, GC])
        ps = k.banks(st, "ps_ssd")
        wx_in = [sem(f"wx_in{c}") for c in range(4)]
        wz_in, tab_in = sem("wz_in"), sem("tab_in")
        ring_mm, ring_ev = sem("ring_mm"), sem("ring_ev")
        conv_ok, xb_ok, tg_ok = sem("conv_ok"), sem("xb_ok"), sem("tg_ok")
        xw_ok, st_mm, scanned = sem("xw_ok"), sem("st_mm"), sem("scanned")
        sr_ok, seg_mm, e_ok = sem("sr_ok"), sem("seg_mm"), sem("e_ok")
        cb_mm, cbm_ok, ec_ok = sem("cb_mm"), sem("cbm_ok"), sem("ec_ok")
        yo_mm, t1_ok, dtx_ok, y_mm = sem("yo_mm"), sem("t1_ok"), sem("dtx_ok"), sem("y_mm")
        s2_ok, u_ok, sq_ok, rs_ok, un_ok = sem("s2_ok"), sem("u_ok"), sem("sq_ok"), sem("rs_ok"), sem("un_ok")
        pads, chain_v, chain_p, chain_a = sem("pads"), sem("chain_v"), sem("chain_p"), sem("chain_a")
        uo_out = [sem(f"uo_out{j}") for j in range(2)]
        block = st.enter_context(nc.Block())

        def tgk(col, c, d):
            o = col + (c * 2 + d) * R
            return tg[:, o:o + R]

        def y_cols(ap):
            return ap.rearrange("p (a q x) -> p a q x", a=R // 2, x=HP)[:, :, 0:4:3]

        def per_head(ap, n=R):
            return ap.rearrange("p (r x) -> p r x", r=n)

        @block.sync
        def _(sp):
            sp.dma_start(conv[:], io["conv"]).then_inc(tab_in, 16)
            sp.dma_start(gains[:], io["ssm_gain"]).then_inc(tab_in, 16)

            def loads(g, first):
                cols = (COL_X + g * GC, COL_X + P + g * GC, COL_B + g * DS, COL_C + g * DS)
                for ct, col in enumerate(cols):
                    if not first:
                        sp.wait_ge(ring_mm, PRIMED + RING * g - RING + min(3 * ct + 3, 11))
                    sp.dma_start(wx[:, ct], w[:, :, bass.ds(col, P)]).then_inc(wx_in[ct], 16)
                if not first:
                    sp.wait_ge(ring_mm, PRIMED + RING * g - RING + 11 + LT // 2)
                sp.dma_start(wz[:], w[:, :, bass.ds(COL_Z + g * GC, GC)]).then_inc(wz_in, 16)
            loads(0, True)
            with sp.Fori(1, GROUPS) as g:
                loads(g, False)

        @block.tensor
        def _(pe):
            for first in (ring_mm, st_mm, seg_mm, y_mm):
                pe.sem_inc(first, PRIMED)
            with pe.Fori(0, GROUPS) as g:
                n = 0

                def ring():
                    pe.wait_ge(ring_ev, PRIMED + RING * g + max(n - 1, 0))
                    return ps[:, n % 2]

                for ct in range(4):
                    pe.wait_ge(wx_in[ct], 16 * g + 16)
                    for _, tok, width in SEGS if ct < 3 else SEGS[1:]:
                        o = ring()
                        for kk in range(KD):
                            ins = pe.matmul(o[:, 0:width], wx[:, ct, kk], hT[:, kk, tok:tok + width],
                                            start=kk == 0, stop=kk == KD - 1)
                        ins.then_inc(ring_mm, 1)
                        n += 1
                pe.wait_ge(wz_in, 16 * g + 16)
                for t in range(0, LT, 2):
                    o = ring()
                    for h in range(2):
                        c0 = NCTX + (t + h) * P
                        for kk in range(KD):
                            ins = pe.matmul(o[:, h * GC:(h + 1) * GC], hT[:, kk, c0:c0 + P], wz[:, kk],
                                            start=kk == 0, stop=kk == KD - 1)
                    ins.then_inc(ring_mm, 1)
                    n += 1
                pe.wait_ge(xb_ok, PRIMED + 4 * g + 4)
                for c in TURN_ORDER:
                    o = ring()
                    c0 = tok_col(c)
                    for ct in range(3):
                        ins = pe.transpose(o[:, ct * P:(ct + 1) * P], xb[:, ct, c0:c0 + P], ident[:])
                    ins.then_inc(ring_mm, 1)
                    n += 1
                for s in range(STEPS):
                    pe.wait_ge(xw_ok, STEPS * g + s + 1)
                    if s < 2:
                        pe.wait_ge(e_ok, PRIMED + LT * g)
                    else:
                        pe.wait_ge(scanned, PRIMED + STEPS * g + s - 1)
                    for d in range(2):
                        ins = pe.matmul(ps[:, 2 + s % 2, d * GC:(d + 1) * GC], tk[:, step_chunk(d, s), GC:GC + DS],
                                        xw[:, s % 2, d], start=True, stop=True)
                    ins.then_inc(st_mm, 1)

                def heads(c):
                    c0 = tok_col(c + CT)
                    pe.wait_ge(sr_ok, LT * g + c + 1)
                    if c < 2:
                        pe.wait_ge(scanned, PRIMED + STEPS * g + STEPS)
                    else:
                        pe.wait_ge(e_ok, PRIMED + LT * g + c - 1)
                    pe.matmul(ps[:, 2 + c % 2], masks[:, SLOW], sr[:, c % 2, 0], start=True, stop=False)
                    pe.matmul(ps[:, 2 + c % 2], masks[:, SUP], sr[:, c % 2, 1], start=False, stop=True).then_inc(seg_mm, 1)
                    pe.wait_ge(cbm_ok, PRIMED + LT * g + c)
                    pe.matmul(ps[:, 4, 0:P], xb[:, 2, c0:c0 + P], xb[:, 3, c0:c0 + P],
                              start=True, stop=True).then_inc(cb_mm, 1)
                    pe.wait_ge(t1_ok, PRIMED + LT * g + c)
                    for d, s in ((0, c + CT - 1), (1, STEPS - 1 - c)):
                        ins = pe.matmul(ps[:, 5, d * GC:(d + 1) * GC], xb[:, 3, c0:c0 + P],
                                        H[:, s, d * GC:(d + 1) * GC], start=True, stop=True)
                    ins.then_inc(yo_mm, 1)

                heads(0)
                for c in range(LT):
                    if c + 1 < LT:
                        heads(c + 1)
                    pe.wait_ge(ec_ok, PRIMED + LT * g + c + 1)
                    pe.wait_ge(dtx_ok, LT * g + c + 1)
                    pe.wait_ge(u_ok, PRIMED + LT * g + max(c - 1, 0))
                    for r in range(R):
                        for d in range(2):
                            ins = pe.matmul(ps[:, 6 + c % 2, r * P:(r + 1) * P], EC[:, c % 2, d, r * P:(r + 1) * P],
                                            dtx[:, c % 2, d, r // 2 * P:(r // 2 + 1) * P], start=d == 0, stop=d == 1)
                    ins.then_inc(y_mm, 1)
                for cc in range(2):
                    for half in range(2):
                        o = ring()
                        pe.wait_ge(un_ok, LT * g + 4 * half + 4)
                        for j in range(4):
                            ins = pe.transpose(o[:, j * P:(j + 1) * P], u[:, 4 * half + j, cc * P:(cc + 1) * P], ident[:])
                        ins.then_inc(ring_mm, 1)
                        n += 1
                assert n == RING

        @block.scalar
        def _(act):
            for first in (ring_ev, xb_ok, e_ok, sq_ok, *uo_out):
                act.sem_inc(first, PRIMED)
            act.wait_ge(pads, 1)
            act.wait_ge(tab_in, 32)
            with act.Fori(0, GROUPS) as g:
                n = 0

                def job():
                    act.wait_ge(ring_mm, PRIMED + RING * g + n + 1)
                    return ps[:, n % 2]

                def to_rows(ct):
                    nonlocal n
                    act.wait_ge(conv_ok, PRIMED + 4 * g + max(ct - 1, 0))
                    for col, _, width in SEGS if ct < 3 else SEGS[1:]:
                        o = job()
                        act.activation(pre[:, ct % 2, PAD + col:PAD + col + width], o[:, 0:width], ACT.Copy).then_inc(ring_ev, 1)
                        n += 1

                def silu(ct):
                    act.wait_ge(conv_ok, PRIMED + 4 * g + ct + 1)
                    act.activation(xb[:, ct], cv[:, ct % 2], ACT.Silu).then_inc(xb_ok, 1)

                def gate(j):
                    nonlocal n
                    o = job()
                    act.activation(u[:, 2 * j:2 * j + 2], o.rearrange("p (t c) -> p t c", t=2), ACT.Silu).then_inc(ring_ev, 1)
                    n += 1

                to_rows(0)
                to_rows(1)
                silu(0)
                to_rows(2)
                silu(1)
                to_rows(3)
                silu(2)
                gate(0)
                gate(1)
                silu(3)
                gate(2)
                gate(3)
                for c in TURN_ORDER:
                    o = job()
                    act.activation(tk[:, c], o[:, 0:GC + DS], ACT.Copy).then_inc(ring_ev, 1)
                    n += 1

                def decay(c):
                    act.wait_ge(seg_mm, PRIMED + LT * g + c + 1)
                    act.wait_ge(ec_ok, PRIMED + LT * g + max(c - 1, 0))
                    act.activation(E[:, c % 2], ps[:, 2 + c % 2], ACT.Exp).then_inc(e_ok, 1)

                decay(0)
                decay(1)
                for c in range(LT):
                    if c + 2 < LT:
                        decay(c + 2)
                    act.wait_ge(u_ok, PRIMED + LT * g + c + 1)
                    act.wait_ge(sq_ok, PRIMED + LT * g + c)
                    act.activation(junk[:], u[:, c], ACT.Square, accum_out=ss[:, 0, c:c + 1]).then_inc(sq_ok, 1)
                act.wait_ge(sq_ok, PRIMED + LT * g + LT)
                act.activation(ss[:, 1], ss[:, 0], ACT.Ln, bias=eps[:], scale=1.0 / GC).then_inc(chain_a, 1)
                act.wait_ge(chain_a, 2 * g + 1)
                act.activation(ss[:, 2], ss[:, 1], ACT.Exp, scale=-0.5).then_inc(rs_ok, 1)
                act.activation(sg[:], gains[:, bass.ds(g, 1)].rearrange("p a c -> p (a c)"), ACT.Copy).then_inc(chain_a, 1)
                act.wait_ge(chain_a, 2 * g + 2)
                for cc in range(2):
                    for half in range(2):
                        j = 2 * cc + half
                        o = job()
                        act.wait_ge(uo_out[j % 2], 32 * g + 16 * (j // 2) + PRIMED)
                        act.activation(uo[:, j % 2], o, ACT.Copy, scale=sg[:, cc:cc + 1]).then_inc(ring_ev, 1)
                        n += 1
                        act.wait_ge(ring_ev, PRIMED + RING * g + n)
                        act.dma_start(io["uT"][bass.ds(2 * g + cc, 1), :, half * 512:half * 512 + 512].rearrange("a p n -> p (a n)"),
                                      uo[:, j % 2]).then_inc(uo_out[j % 2], 16)
                assert n == RING
            for j in range(2):
                act.wait_ge(uo_out[j], 32 * GROUPS + PRIMED)

        @block.vector
        def _(dve):
            for first in (conv_ok, scanned, cbm_ok, ec_ok, t1_ok, u_ok):
                dve.sem_inc(first, PRIMED)
            step = Chain(dve, chain_v)
            for b in range(2):
                for c0 in (0, PAD + NCTX, CONVN + PAD):
                    step(dve.memset(pre[:, b, c0:c0 + PAD], 0.0))
            dve.memset(cv[:, 0, 0:1], 0.0).then_inc(pads, 1)
            dve.wait_ge(pads, 1)
            dve.wait_ge(tab_in, 32)
            with dve.Fori(0, GROUPS) as g:
                step.loop(g, STEPS_V)
                step(dve.tensor_copy(cg[:], conv[:, bass.ds(g, 1)].rearrange("p a c t -> p (a c) t")))
                for ct in range(4):
                    dve.wait_ge(ring_ev, PRIMED + RING * g + min(3 * ct + 3, 11))
                    dve.wait_ge(xb_ok, PRIMED + 4 * g + max(ct - 1, 0))
                    row, out = pre[:, ct % 2], cv[:, ct % 2]
                    step(dve.tensor_scalar(out, row[:, 0:CONVN], cg[:, ct, 0:1], cg[:, ct, TAPS:TAPS + 1], ALU.mult, ALU.add))
                    for tap in range(1, TAPS):
                        ins = dve.scalar_tensor_tensor(out, row[:, tap:tap + CONVN], cg[:, ct, tap:tap + 1], out, ALU.mult, ALU.add)
                        if tap < TAPS - 1:
                            step(ins)
                    ins.then_inc(conv_ok, 1)
                dve.wait_ge(s2_ok, PRIMED + LT * g)
                dve.tensor_copy(tg[:], tab[:, bass.ds(g, 1)].rearrange("p a n -> p (a n)")).then_inc(tg_ok, 1)
                dve.wait_ge(tg_ok, g + 1)
                for s in range(STEPS):
                    dve.wait_ge(st_mm, PRIMED + STEPS * g + s + 1)
                    new = ps[:, 2 + s % 2]
                    if s == 0:
                        dve.tensor_copy(H[:, 0], new).then_inc(scanned, 1)
                    else:
                        dve.wait_ge(scanned, PRIMED + STEPS * g + s)
                        step(dve.tensor_tensor(per_head(H[:, s], 2 * R), per_head(H[:, s - 1], 2 * R),
                                               bcast(tg[:, T_CD + s * 2 * R:T_CD + (s + 1) * 2 * R].unsqueeze(2), 2 * R, HP), ALU.mult))
                        dve.tensor_tensor(H[:, s], H[:, s], new, ALU.add).then_inc(scanned, 1)

                def gated(c):
                    dve.wait_ge(y_mm, PRIMED + LT * g + c + 1)
                    dve.wait_ge(s2_ok, PRIMED + LT * g + c + 1)
                    four = lambda a: a.rearrange("p (a q x) -> p a q x", a=R // 2, x=HP)
                    step(dve.tensor_tensor(four(t1[:, c % 2, 1]), y_cols(ps[:, 6 + c % 2]), four(t1[:, c % 2, 0]), ALU.add))
                    dve.tensor_tensor(u[:, c], u[:, c], t1[:, c % 2, 1], ALU.mult).then_inc(u_ok, 1)

                for c in range(LT):
                    dve.wait_ge(cb_mm, LT * g + c + 1)
                    dve.wait_ge(ec_ok, PRIMED + LT * g + c)
                    dve.tensor_tensor(cbm[:], bcast(ps[:, 4, 0:P].unsqueeze(1), 2, P), masks[:, UP:LOW + 1], ALU.mult).then_inc(cbm_ok, 1)
                    dve.wait_ge(cbm_ok, PRIMED + LT * g + c + 1)
                    dve.wait_ge(e_ok, PRIMED + LT * g + c + 1)
                    dve.wait_ge(y_mm, PRIMED + LT * g + max(c - 1, 0))
                    for d in range(2):
                        ins = dve.tensor_tensor(per_head(EC[:, c % 2, d]), per_head(E[:, c % 2]),
                                                bcast(cbm[:, d].unsqueeze(1), R, P), ALU.mult)
                    ins.then_inc(ec_ok, 1)
                    dve.wait_ge(yo_mm, LT * g + c + 1)
                    if c >= 2:
                        dve.wait_ge(u_ok, PRIMED + LT * g + c - 1)
                    o = T_EA + (c + CT) * 2 * R
                    dve.tensor_tensor(t1[:, c % 2].rearrange("p d (r x) -> p (d r) x", r=R), per_head(ps[:, 5], 2 * R),
                                      bcast(tg[:, o:o + 2 * R].unsqueeze(2), 2 * R, HP), ALU.mult).then_inc(t1_ok, 1)
                    if c >= 1:
                        gated(c - 1)
                gated(LT - 1)
                dve.wait_ge(rs_ok, g + 1)
                for c in range(LT):
                    dve.tensor_scalar(u[:, c], u[:, c], ss[:, 2, c:c + 1], None, ALU.mult).then_inc(un_ok, 1)
            step.leave(GROUPS)

        @block.gpsimd
        def _(pool):
            pool.sem_inc(s2_ok, PRIMED)
            step = Chain(pool, chain_p)
            with pool.Fori(0, GROUPS) as g:
                step.loop(g, STEPS_P)
                pool.wait_ge(tg_ok, g + 1)
                for s in range(STEPS):
                    pool.wait_ge(ring_ev, PRIMED + RING * g + 11 + LT // 2 + (2 if s < 2 else min(2 * s, NT)))
                    pool.wait_ge(st_mm, PRIMED + STEPS * g + max(s - 1, 0))
                    for d in range(2):
                        c = step_chunk(d, s)
                        ins = pool.tensor_tensor(per_head(xw[:, s % 2, d]), per_head(tk[:, c, 0:GC]),
                                                 bcast(tgk(T_WEND, c, d).unsqueeze(2), R, HP), ALU.mult)
                    ins.then_inc(xw_ok, 1)

                def ahead(c):
                    pool.wait_ge(seg_mm, PRIMED + LT * g + max(c - 1, 0))
                    for d, m in ((0, UP), (1, LOW)):
                        ins = pool.tensor_tensor(per_head(sr[:, c % 2, d]), bcast(tgk(T_DA, c + CT, d).unsqueeze(2), R, P),
                                                 bcast(masks[:, m].unsqueeze(1), R, P), ALU.mult)
                    ins.then_inc(sr_ok, 1)
                    pool.wait_ge(y_mm, PRIMED + LT * g + max(c - 1, 0))
                    for d in range(2):
                        ins = pool.tensor_tensor(per_head(dtx[:, c % 2, d]), per_head(tk[:, c + CT, 0:GC]),
                                                 bcast(tgk(T_DT, c + CT, d).unsqueeze(2), R, HP), ALU.mult)
                    ins.then_inc(dtx_ok, 1)

                ahead(0)
                for c in range(LT):
                    if c + 1 < LT:
                        ahead(c + 1)
                    step(pool.tensor_tensor(per_head(xd[:]), per_head(tk[:, c + CT, 0:GC]),
                                            bcast(tg[:, T_SKIP:T_ALL].unsqueeze(2), R, HP), ALU.mult))
                    pool.wait_ge(t1_ok, PRIMED + LT * g + c + 1)
                    step(pool.tensor_tensor(xd[:], xd[:], t1[:, c % 2, 0], ALU.add))
                    pool.tensor_tensor(t1[:, c % 2, 0], xd[:], t1[:, c % 2, 1], ALU.add).then_inc(s2_ok, 1)
                    pool.wait_ge(s2_ok, PRIMED + LT * g + c + 1)
            step.leave(GROUPS)


STEPS_V = 1 + 4 * (TAPS - 1) + STEPS - 1 + LT
STEPS_P = 2 * LT


def compress(k, keep, hT, cqT, ckvT, kst):
    nc, io = k.nc, k.io
    ident, eps = keep["ident"], keep["eps"]
    with ExitStack() as st:
        sb = lambda n, s: k.sb(st, n, s)
        wc = sb("wc", [P, KD, NC_SMALL])
        cs = sb("cs", [P, NT, NC_SMALL])
        junk = sb("junk_c", [P, QL])
        ss = sb("ss_c", [P, 3, 3, NT])
        gT = sb("gT", [P, 3])
        gr = sb("gr", [P, ROPE])
        rope = sb("rope_c", [P, 2, LT, ROPE])
        kr = sb("kr", [P, NT, ROPE])
        ka = sb("ka", [P, LT, ROPE])
        kb = sb("kb", [P, LT, ROPE])
        ps = k.banks(st, "ps_c")
        sem = lambda n: k.sem(st, "c_" + n)
        w_in, par_in, mm, ev, stat, rs_ok, sc_ok, turned, out_ok, chain = (
            sem(n) for n in ("w_in", "par_in", "mm", "ev", "stat", "rs_ok", "sc_ok", "turned", "out_ok", "chain"))
        block = st.enter_context(nc.Block())
        kinds = ((0, QL), (QL, QL + KVL), (QL + KVL, NC_SMALL))

        @block.sync
        def _(sp):
            sp.dma_start(wc[:], io["w_in"][0].rearrange("(k p) n -> p k n", p=P)[:, :, 0:NC_SMALL]).then_inc(w_in, 16)
            for dst, src in ((gT[:, 0:2], io["q_gain"]), (gT[:, 2:3], io["kv_gain"]), (rope[:], io["rope"]),
                             (gr[:], io["qk_k_g"][0, NOPE:QKD].partition_broadcast(P))):
                sp.dma_start(dst, src).then_inc(par_in, 16)

        @block.tensor
        def _(pe):
            pe.wait_ge(w_in, 16)
            for t in range(NT):
                if t >= 4:
                    pe.wait_ge(ev, t - 3)
                lo = QL if t < CT else 0
                for kk in range(KD):
                    ins = pe.matmul(ps[:, t % 4, lo:NC_SMALL], hT[:, kk, t * P:(t + 1) * P], wc[:, kk, lo:],
                                    start=kk == 0, stop=kk == KD - 1)
                ins.then_inc(mm, 1)
            for t in range(NT):
                pe.wait_ge(sc_ok, t + 1)
                if t >= 4:
                    pe.wait_ge(out_ok, t - 3)
                for j in range(2 if t < CT else 0, 3):
                    ins = pe.transpose(ps[:, 4 + t % 4, j * P:(j + 1) * P], cs[:, t, j * P:(j + 1) * P], ident[:])
                ins.then_inc(turned, 1)

        @block.scalar
        def _(act):
            step = Chain(act, stat)
            for t in range(NT):
                lo = QL if t < CT else 0
                act.wait_ge(mm, t + 1)
                act.activation(cs[:, t, lo:], ps[:, t % 4, lo:NC_SMALL], ACT.Copy).then_inc(ev, 1)
                act.wait_ge(ev, t + 1)
                for j, (a, b) in enumerate(kinds):
                    if j > 0 or t >= CT:
                        step(act.activation(junk[:, 0:b - a], cs[:, t, a:b], ACT.Square, accum_out=ss[:, 0, j, t:t + 1]))
            for j, (a, b) in enumerate(kinds):
                lo = CT if j == 0 else 0
                step(act.activation(ss[:, 1, j, lo:], ss[:, 0, j, lo:], ACT.Ln, bias=eps[:], scale=1.0 / (b - a)))
            act.activation(ss[:, 2, 0, CT:], ss[:, 1, 0, CT:], ACT.Exp, scale=-0.5).then_inc(rs_ok, 1)
            act.activation(ss[:, 2, 1:3], ss[:, 1, 1:3], ACT.Exp, scale=-0.5).then_inc(rs_ok, 1)
            act.wait_ge(par_in, 64)
            for t in range(NT):
                act.wait_ge(turned, t + 1)
                for j in range(2 if t < CT else 0, 3):
                    dst = ckvT[:, t * P:(t + 1) * P] if j == 2 else cqT[:, j, (t - CT) * P:(t - CT + 1) * P]
                    ins = act.activation(dst, ps[:, 4 + t % 4, j * P:(j + 1) * P], ACT.Copy, scale=gT[:, j:j + 1])
                ins.then_inc(out_ok, 1)

        @block.vector
        def _(dve):
            step = Chain(dve, chain)
            dve.wait_ge(rs_ok, 2)
            for t in range(NT):
                if t >= CT:
                    dve.tensor_scalar(cs[:, t, 0:QL], cs[:, t, 0:QL], ss[:, 2, 0, t:t + 1], None, ALU.mult)
                dve.tensor_scalar(cs[:, t, QL:QL + KVL], cs[:, t, QL:QL + KVL], ss[:, 2, 1, t:t + 1], None, ALU.mult).then_inc(sc_ok, 1)
            dve.wait_ge(par_in, 64)
            step(dve.tensor_tensor(kr[:], cs[:, :, QL + KVL:], bcast(ss[:, 2, 2].unsqueeze(2), NT, ROPE), ALU.mult))
            step(dve.tensor_tensor(kr[:], kr[:], bcast(gr[:].unsqueeze(1), NT, ROPE), ALU.mult))
            step(dve.tensor_tensor(ka[:], kr[:, CT:], rope[:, 0], ALU.mult))
            halves = lambda a: a.rearrange("p t (x h y) -> p (t x) h y", x=2, h=2)
            for h in range(2):
                step(dve.tensor_tensor(halves(kb[:])[:, :, h], halves(kr[:, CT:])[:, :, 1 - h], halves(rope[:, 1])[:, :, h], ALU.mult))
            for h in range(2):
                dve.tensor_copy(kst[:, 0:CT, h, NOPE:], kr[:, 0:CT])
                step(dve.tensor_tensor(kst[:, CT:, h, NOPE:], ka[:], kb[:], ALU.add))


KEY_SEGS = ((0, 512), (512, 512), (1024, 256))
TILES = 2 * LT


class Bank:

    def __init__(self, full, empty, at):
        self.full, self.empty, self.at = full, empty, at

    def fill(self, pe):
        pe.wait_ge(self.empty.sem, self.empty.value())
        return self.at

    def filled(self, ins):
        self.full.raised(ins)
        self.empty.add()

    def take(self, eng):
        eng.wait_ge(self.full.sem, self.full.add())
        return self.at

    def emptied(self, ins):
        self.empty.raised(ins)

    def skip(self, n=1):
        self.full.add(n)
        self.empty.add(n)


def attention(k, keep, hT, cqT, ckvT, kst, attT):
    nc, io = k.nc, k.io
    ident, eps = keep["ident"], keep["eps"]
    QW, KW = 2 * QKD, 2 * (NOPE + VD)
    with ExitStack() as st:
        sb = lambda n, s: k.sb(st, n, s)
        sem = lambda n: k.sem(st, "a_" + n)
        wq = sb("wq", [P, 2, 2, QW])
        wkv = sb("wkv", [P, 2, KW])
        q = sb("q", [P, LT, QW])
        kv = sb("kv", [P, 2, NT, KW])
        sq = sb("sq", [P, LT * QW])
        rope = sb("rope_a", [P, 2, LT, ROPE])
        qa = sb("qa", [P, LT, 2, ROPE])
        qb = sb("qb", [P, LT, 2, ROPE])
        gr = sb("gr_a", [P, ROPE])
        gT = sb("gT_a", [P, 2])
        ss = sb("ss_a", [P, 3, 4 * LT + 2 * NT])
        QT = sb("QT", [P, 2, 2, NLAT])
        KT = sb("KT", [P, 2, 2, NTOK])
        pr = sb("pr", [P, 2, NTOK])
        pT = sb("pT", [P, 2, NT, P])
        att = sb("att", [P, LT, 2, VD])
        mx = sb("mx", [P, 4, TILES])
        ps = k.banks(st, "ps_a")
        w_in = [sem(f"w_in{b}") for b in range(2)]
        par_in, one_ok = sem("par_in"), sem("one_ok")
        full = [sem("full6"), sem("full7")]
        empty = [sem("empty6"), sem("empty7")]
        sqq, redq, sqk, redk, rs_ok, qk_ok = (sem(n) for n in ("sqq", "redq", "sqk", "redk", "rs_ok", "qk_ok"))
        s_mm, mx_ok, nb_ok, exp_ok, pv_ok = (sem(n) for n in ("s_mm", "mx_ok", "nb_ok", "exp_ok", "pv_ok"))
        turn_ok, chain_v, chain_a = sem("turn_ok"), sem("chain_v"), sem("chain_a")
        block = st.enter_context(nc.Block())
        NQ, NK = 2 * LT, 2 * NT
        cut_q, cut_k, cut_r = slice(0, NQ), slice(NQ, NQ + NK), slice(NQ + NK, 2 * NQ + NK)

        def banks():
            return [Bank(Count(full[j]), Count(empty[j]), ps[:, 6 + j]) for j in range(2)]

        proj = [("q", t) for t in range(0, LT, 2)] + [("kv", t) for t in range(0, NT, 2)]
        turns = [("q", h, t, 4) for h in range(2) for t in range(0, LT, 4)] + \
                [("k", h, t, min(4, NT - t)) for h in range(2) for t in range(0, NT, 4)]

        class Walk:

            def __init__(self, loops):
                self.loops = loops

            def pair(self, p, b, more):
                for m in range(TILES + 3):
                    self.tile(p, b, m)
                    if m == 1 and more:
                        self.project(1 - b)
                    if m == 4 and more:
                        self.reduce(1 - b)
                    if m == 6 and more:
                        self.scale(1 - b)
                    if m == 9 and more:
                        self.turn(1 - b)
                self.store(p, b)

            def all(self, eng):
                self.project(0)
                self.reduce(0)
                self.scale(0)
                self.turn(0)
                turns_ = PAIRS // 2 - 1
                with eng.Fori(0, turns_) as i:
                    for c, per in self.loops:
                        c.loop(i, per)
                    self.pair(2 * i, 0, True)
                    self.pair(2 * i + 1, 1, True)
                for c, _ in self.loops:
                    c.leave(turns_)
                self.pair(PAIRS - 2, 0, True)
                self.pair(PAIRS - 1, 1, False)

            def reduce(self, b):
                pass

            def scale(self, b):
                pass

            def tile(self, p, b, m):
                pass

            def store(self, p, b):
                pass

        JOBS = (2 * (2 * TILES + 5 + 5 + 1), 2 * (2 * TILES + 4 + 5 + 1))

        @block.sync
        def _(sp):
            def loads(p, b):
                sp.dma_start(wq[:, b], io["w_uq"][0].rearrange("(k p) n -> p k n", p=P)[:, :, bass.ds(p * QW, QW)]).then_inc(w_in[b], 16)
                sp.wait_ge(w_in[b], 32 * (p // 2) + 16 if isinstance(p, int) else 16 * (p - b) + 16)
                sp.dma_start(wkv[:, b], io["w_ukv"][0, :, bass.ds(p * KW, KW)]).then_inc(w_in[b], 16)

            sp.dma_start(rope[:], io["rope"]).then_inc(par_in, 16)
            sp.dma_start(gr[:], io["qk_q_g"][0, NOPE:QKD].partition_broadcast(P)).then_inc(par_in, 16)
            sp.wait_ge(one_ok, 1)
            sp.dma_start(gT[0:NOPE, :], io["qk_gain"][0:NOPE]).then_inc(par_in, 16)
            loads(0, 0)
            loads(1, 1)
            with sp.Fori(1, PAIRS // 2) as i:
                for b in range(2):
                    sp.wait_ge(qk_ok, 2 * i + b - 1)
                    loads(2 * i + b, b)

        @block.tensor
        def _(pe):
            bk = banks()
            sm, ex, qk = Count(s_mm), Count(exp_ok, primed=PRIMED), Count(qk_ok)
            wi = [Count(w_in[b], 32) for b in range(2)]

            class Pe(Walk):
                def project(self, b):
                    pe.wait_ge(w_in[b], wi[b].add())
                    for n, (kind, t) in enumerate(proj):
                        o = bk[n % 2].fill(pe)
                        for h in range(2):
                            if kind == "q":
                                for kk in range(2):
                                    ins = pe.matmul(o[:, h * QW:(h + 1) * QW], cqT[:, kk, (t + h) * P:(t + h + 1) * P],
                                                    wq[:, b, kk], start=kk == 0, stop=kk == 1)
                            else:
                                ins = pe.matmul(o[:, h * KW:(h + 1) * KW], ckvT[:, (t + h) * P:(t + h + 1) * P],
                                                wkv[:, b], start=True, stop=True)
                        bk[n % 2].filled(ins)

                def turn(self, b):
                    pe.wait_ge(qk_ok, qk.add())
                    for n, (kind, h, t, cnt) in enumerate(turns):
                        o = bk[n % 2].fill(pe)
                        for j in range(cnt):
                            src = q[:, t + j, h * QKD:(h + 1) * QKD] if kind == "q" else kst[:, t + j, h]
                            ins = pe.transpose(o[0:QKD, j * P:(j + 1) * P], src, ident[:])
                        bk[n % 2].filled(ins)

                def tile(self, p, b, m):
                    if m < TILES + 2:
                        pe.wait_ge(exp_ok, exv(m - 2) if m >= 2 else exv(-1))
                    for j, (c0, wd) in enumerate(KEY_SEGS):
                        if m < TILES:
                            h, t = m // LT, m % LT
                            ins = pe.matmul(ps[:, 3 * (m % 2) + j, 0:wd], QT[0:QKD, b, h, t * P:(t + 1) * P],
                                            KT[0:QKD, b, h, c0:c0 + wd], start=True, stop=True)
                            if j == 2:
                                sm.raised(ins)
                        if 2 <= m < TILES + 2:
                            o = bk[j % 2].fill(pe)
                            for c in range(c0 // P, (c0 + wd) // P):
                                ins = pe.transpose(o[:, c * P - c0:c * P - c0 + P], pr[:, m % 2, c * P:(c + 1) * P], ident[:])
                            bk[j % 2].filled(ins)
                    if m >= 3:
                        n = m - 3
                        o = bk[1].fill(pe)
                        pe.wait_ge(bk[0].empty.sem, bk[0].empty.value(2 if m < TILES + 2 else 0))
                        for c in range(NT):
                            ins = pe.matmul(o[:, 0:VD], pT[:, n % 2, c], kv[:, b, c, (n // LT) * (NOPE + VD) + NOPE:(n // LT + 1) * (NOPE + VD)],
                                            start=c == 0, stop=c == NT - 1)
                        bk[1].filled(ins)

                def store(self, p, b):
                    ex.add(TILES)
                    pe.wait_ge(bk[1].empty.sem, bk[1].empty.value())
                    for j in range(2):
                        o = bk[j].fill(pe)
                        for t in range(4):
                            ins = pe.transpose(o[:, t * P:(t + 1) * P], att[:, 4 * j + t].rearrange("p h x -> p (h x)"), ident[:])
                        bk[j].filled(ins)

            def exv(n):
                return ex.value() + (n + 1)

            walk = Pe([(bk[0].full, JOBS[0]), (bk[0].empty, JOBS[0]), (bk[1].full, JOBS[1]), (bk[1].empty, JOBS[1]),
                       (sm, 2 * TILES), (ex, 2 * TILES), (qk, 2), (wi[0], 1), (wi[1], 1)])
            walk.all(pe)

        @block.scalar
        def _(act):
            bk = banks()
            nb, rk, rq = Count(nb_ok), Count(redk), Count(redq)
            ex, rs = Count(exp_ok, primed=PRIMED), Count(rs_ok)
            act.sem_inc(exp_ok, PRIMED)
            step = Chain(act, chain_a)
            act.wait_ge(par_in, 48)

            class Act(Walk):
                def project(self, b):
                    for n, (kind, t) in enumerate(proj):
                        if n % 2:
                            bk[1].skip()
                            continue
                        o = bk[0].take(act)
                        dst, wd = (q[:, t:t + 2], QW) if kind == "q" else (kv[:, b, t:t + 2], KW)
                        bk[0].emptied(act.activation(dst, o[:, 0:2 * wd].rearrange("p (t n) -> p t n", t=2), ACT.Copy))

                def scale(self, b):
                    act.wait_ge(redk, rk.add())
                    step(act.activation(ss[:, 1, 0:NQ + NK], ss[:, 0, 0:NQ + NK], ACT.Ln, bias=eps[:], scale=1.0 / NOPE))
                    step(act.activation(ss[:, 1, cut_r], ss[:, 0, cut_r], ACT.Ln, bias=eps[:], scale=1.0 / ROPE))
                    rs.raised(act.activation(ss[:, 2], ss[:, 1], ACT.Exp, scale=-0.5))

                def turn(self, b):
                    for n, (kind, h, t, cnt) in enumerate(turns):
                        if n % 2:
                            bk[1].skip()
                            continue
                        o = bk[0].take(act)
                        dst, g = (QT, 0) if kind == "q" else (KT, 1)
                        bk[0].emptied(act.activation(dst[0:QKD, b, h, t * P:(t + cnt) * P], o[0:QKD, 0:cnt * P], ACT.Copy,
                                                     scale=gT[0:QKD, g:g + 1]))

                def tile(self, p, b, m):
                    if 2 <= m < TILES + 2:
                        self.evac(m, 0)
                        self.evac(m, 2)
                        bk[1].skip()
                    if m < TILES:
                        act.wait_ge(nb_ok, nb.add())
                        ex.raised(act.activation(pr[:, m % 2], ps[:, 3 * (m % 2):3 * (m % 2) + 3].rearrange("p b n -> p (b n)")[:, 0:NTOK],
                                                 ACT.Exp, bias=mx[:, 1, m:m + 1], scale=SCALE, accum_out=mx[:, 2, m:m + 1]))
                    if m >= 3:
                        bk[1].skip()

                def evac(self, m, j):
                    c0, wd = KEY_SEGS[j]
                    o = bk[0].take(act)
                    bk[0].emptied(act.activation(pT[:, m % 2, c0 // P:(c0 + wd) // P], o[:, 0:wd].rearrange("p (c n) -> p c n", n=P), ACT.Copy))

                def store(self, p, b):
                    o = bk[0].take(act)
                    bk[0].emptied(act.activation(attT[:, bass.ds(p, 1), 0:512].rearrange("p a n -> p (a n)"), o, ACT.Copy))
                    bk[1].skip()

            walk = Act([(bk[0].full, JOBS[0]), (bk[0].empty, JOBS[0]), (bk[1].full, JOBS[1]), (bk[1].empty, JOBS[1]),
                        (nb, 2 * TILES), (ex, 2 * TILES), (rk, 2), (rs, 2), (step, 4)])
            walk.all(act)

        @block.vector
        def _(dve):
            bk = banks()
            sm, ex, rs = Count(s_mm), Count(exp_ok, primed=PRIMED), Count(rs_ok)
            sq1, sq2, r1, r2, qk, nb = Count(sqq), Count(sqk), Count(redq), Count(redk), Count(qk_ok), Count(nb_ok)
            step = Chain(dve, chain_v)
            dve.memset(gT[:], 1.0).then_inc(one_ok, 1)
            dve.wait_ge(par_in, 48)

            class Dve(Walk):
                def project(self, b):
                    for n, (kind, t) in enumerate(proj):
                        if n % 2 == 0:
                            bk[0].skip()
                            continue
                        o = bk[1].take(dve)
                        dst, wd = (q[:, t:t + 2], QW) if kind == "q" else (kv[:, b, t:t + 2], KW)
                        bk[1].emptied(dve.tensor_copy(dst, o[:, 0:2 * wd].rearrange("p (t n) -> p t n", t=2)))

                def reduce(self, b):
                    dve.wait_ge(sqq, sq1.add())
                    rows = sq[:].rearrange("p (n x) -> p n x", x=QKD)
                    dve.tensor_reduce(ss[:, 0, cut_q], rows[:, :, 0:NOPE], AX_X, ALU.add)
                    r1.raised(dve.tensor_reduce(ss[:, 0, cut_r], rows[:, :, NOPE:], AX_X, ALU.add))
                    dve.wait_ge(sqk, sq2.add())
                    r2.raised(dve.tensor_reduce(ss[:, 0, cut_k], sq[:, 0:NK * NOPE].rearrange("p (n x) -> p n x", x=NOPE), AX_X, ALU.add))

                def scale(self, b):
                    dve.wait_ge(rs_ok, rs.add())
                    rows = q[:].rearrange("p t (h x) -> p (t h) x", h=2)
                    turn = rows[:, :, NOPE:]
                    dve.tensor_tensor(rows[:, :, 0:NOPE], rows[:, :, 0:NOPE], bcast(ss[:, 2, cut_q].unsqueeze(2), NQ, NOPE), ALU.mult)
                    step(dve.tensor_tensor(turn, turn, bcast(ss[:, 2, cut_r].unsqueeze(2), NQ, ROPE), ALU.mult))
                    step(dve.tensor_tensor(turn, turn, bcast(gr[:].unsqueeze(1), NQ, ROPE), ALU.mult))
                    q4 = q[:].rearrange("p t (h x) -> p t h x", h=2)[:, :, :, NOPE:]
                    dve.tensor_tensor(qa[:], q4, bcast(rope[:, 0].unsqueeze(2), LT, 2, ROPE), ALU.mult)
                    halves = lambda a: a.rearrange("p t (x h y) -> p t x h y", x=2, h=2)
                    for h in range(2):
                        for e in range(2):
                            ins = dve.tensor_tensor(halves(qb[:, :, h])[:, :, :, e], halves(q4[:, :, h])[:, :, :, 1 - e],
                                                    halves(rope[:, 1])[:, :, :, e], ALU.mult)
                    step(ins)
                    dve.tensor_tensor(turn, qa[:].rearrange("p t h x -> p (t h) x"), qb[:].rearrange("p t h x -> p (t h) x"), ALU.add)
                    kn = kst[:].rearrange("p t h x -> p (t h) x")[:, :, 0:NOPE]
                    qk.raised(dve.tensor_tensor(kn, kv[:, b].rearrange("p t (h x) -> p (t h) x", h=2)[:, :, 0:NOPE],
                                                bcast(ss[:, 2, cut_k].unsqueeze(2), NK, NOPE), ALU.mult))

                def turn(self, b):
                    for n, (kind, h, t, cnt) in enumerate(turns):
                        if n % 2 == 0:
                            bk[0].skip()
                            continue
                        o = bk[1].take(dve)
                        dst, g = (QT, 0) if kind == "q" else (KT, 1)
                        bk[1].emptied(dve.tensor_scalar(dst[0:QKD, b, h, t * P:(t + cnt) * P], o[0:QKD, 0:cnt * P],
                                                        gT[0:QKD, g:g + 1], None, ALU.mult))

                def tile(self, p, b, m):
                    if 2 <= m < TILES + 2:
                        c0, wd = KEY_SEGS[1]
                        o = bk[1].take(dve)
                        bk[1].emptied(dve.tensor_copy(pT[:, m % 2, c0 // P:(c0 + wd) // P], o[:, 0:wd].rearrange("p (c n) -> p c n", n=P)))
                        bk[0].skip(2)
                    if m < TILES:
                        dve.wait_ge(s_mm, sm.add())
                        step(dve.tensor_reduce(mx[:, 0, m:m + 1], ps[:, 3 * (m % 2):3 * (m % 2) + 3].rearrange("p b n -> p (b n)")[:, 0:NTOK],
                                               AX_X, ALU.max))
                        nb.raised(dve.tensor_scalar(mx[:, 1, m:m + 1], mx[:, 0, m:m + 1], -SCALE, None, ALU.mult))
                    if m >= 3:
                        n = m - 3
                        dve.wait_ge(exp_ok, ex.add())
                        step(dve.reciprocal(mx[:, 3, n:n + 1], mx[:, 2, n:n + 1]))
                        o = bk[1].take(dve)
                        bk[1].emptied(dve.tensor_scalar(att[:, n % LT, n // LT], o[:, 0:VD], mx[:, 3, n:n + 1], None, ALU.mult))

                def store(self, p, b):
                    o = bk[1].take(dve)
                    bk[1].emptied(dve.tensor_copy(attT[:, bass.ds(p, 1), 512:1024].rearrange("p a n -> p (a n)"), o))
                    bk[0].skip()

            walk = Dve([(bk[0].full, JOBS[0]), (bk[0].empty, JOBS[0]), (bk[1].full, JOBS[1]), (bk[1].empty, JOBS[1]),
                        (sm, 2 * TILES), (ex, 2 * TILES), (nb, 2 * TILES), (rs, 2), (sq1, 2), (sq2, 2), (r1, 2), (r2, 2), (qk, 2),
                        (step, 2 * (2 * TILES + 3))])
            walk.all(dve)

        @block.gpsimd
        def _(pool):
            bk = banks()
            s1, s2, r1 = Count(sqq), Count(sqk), Count(redq)

            class Pool(Walk):
                def project(self, b):
                    bk[0].skip(5)
                    bk[1].skip(4)
                    for j in range(2):
                        pool.wait_ge(bk[j].empty.sem, bk[j].empty.value())
                    s1.raised(pool.tensor_tensor(sq[:], q[:].rearrange("p t x -> p (t x)"), q[:].rearrange("p t x -> p (t x)"), ALU.mult))
                    pool.wait_ge(redq, r1.add())
                    kn = kv[:, b].rearrange("p t (h x) -> p (t h) x", h=2)[:, :, 0:NOPE]
                    s2.raised(pool.tensor_tensor(sq[:, 0:NK * NOPE].rearrange("p (n x) -> p n x", x=NOPE), kn, kn, ALU.mult))

                def turn(self, b):
                    bk[0].skip(5)
                    bk[1].skip(5)

                def tile(self, p, b, m):
                    if 2 <= m < TILES + 2:
                        bk[0].skip(2)
                        bk[1].skip(1)
                    if m >= 3:
                        bk[1].skip(1)

                def store(self, p, b):
                    bk[0].skip()
                    bk[1].skip()

            walk = Pool([(bk[0].full, JOBS[0]), (bk[0].empty, JOBS[0]), (bk[1].full, JOBS[1]), (bk[1].empty, JOBS[1]), (s1, 2), (s2, 2), (r1, 2)])
            walk.all(pool)


def merge(k, keep, hT, attT, uT, mT):
    nc, io = k.nc, k.io
    w = io["w_in"][0].rearrange("(k p) n -> p k n", p=P)
    wab = io["w_late"].rearrange("(k p) n -> p k n", p=P)
    wa, wb = wab[:, KD:2 * KD], wab[:, 2 * KD:]
    with ExitStack() as st:
        sem = lambda n: k.sem(st, "g_" + n)
        ws = k.sb(st, "ws", [P, 5, KD, P])
        sig = k.sb(st, "sig", [P, 2, 2, 512])
        ps = k.banks(st, "ps_m")
        w_in = [sem(f"w_in{j}") for j in range(5)]
        u_in = [sem(f"u_in{j}") for j in range(4)]
        mm, sig_ok, prod, merged = sem("mm"), sem("sig_ok"), sem("prod"), sem("merged")
        block = st.enter_context(nc.Block())

        @block.sync
        def _(sp):
            def loads(m, first):
                for j, (src, col, done) in enumerate(((w, COL_GA, 2), (w, COL_GB, 4), (wa, 0, 6), (wb[:, 0:KD], 0, 8), (wb[:, KD:], 0, 8))):
                    if not first:
                        sp.wait_ge(mm, 8 * m - 8 + done)
                    sp.dma_start(ws[:, j], src[:, :, bass.ds(col + m * P, P)]).then_inc(w_in[j], 16)
            loads(0, True)
            for j in range(4):
                sp.dma_start(uT[:, 4 * j:4 * j + 4], io["uT"][4 * j:4 * j + 4].rearrange("t p n -> p t n")).then_inc(u_in[j], 16)
            with sp.Fori(0, KD - 1) as m:
                loads(m + 1, False)

        @block.tensor
        def _(pe):
            with pe.Fori(0, KD) as m:
                for kind in range(4):
                    pe.wait_ge(w_in[kind], 16 * m + 16)
                    if kind == 3:
                        pe.wait_ge(w_in[4], 16 * m + 16)
                        for j in range(4):
                            pe.wait_ge(u_in[j], 16)
                    for half in range(2):
                        if kind < 2:
                            pe.wait_ge(sig_ok, PRIMED + 4 * m)
                        else:
                            pe.wait_ge(prod, PRIMED + 4 * m)
                        o = ps[:, 2 * kind + half]
                        cols = slice(half * 512, half * 512 + 512)
                        for kk in range(2 * KD if kind == 3 else KD):
                            lhs = ws[:, kind + kk // KD, kk % KD]
                            rhs = (hT[:, kk, NCTX + half * 512:NCTX + half * 512 + 512] if kind < 2 else
                                   attT[:, kk, cols] if kind == 2 else uT[:, kk, cols])
                            ins = pe.matmul(o, lhs, rhs, start=kk == 0, stop=kk == (2 * KD if kind == 3 else KD) - 1)
                        ins.then_inc(mm, 1)

        @block.scalar
        def _(act):
            act.sem_inc(sig_ok, PRIMED)
            with act.Fori(0, KD) as m:
                act.wait_ge(merged, PRIMED + 2 * m)
                for kind in range(2):
                    for half in range(2):
                        act.wait_ge(mm, 8 * m + 2 * kind + half + 1)
                        act.activation(sig[:, kind, half], ps[:, 2 * kind + half], ACT.Sigmoid).then_inc(sig_ok, 1)

        @block.vector
        def _(dve):
            dve.sem_inc(prod, PRIMED)
            with dve.Fori(0, KD) as m:
                for kind in range(2):
                    for half in range(2):
                        dve.wait_ge(mm, 8 * m + 4 + 2 * kind + half + 1)
                        dve.wait_ge(sig_ok, PRIMED + 4 * m + 2 * kind + half + 1)
                        dve.tensor_tensor(sig[:, kind, half], ps[:, 4 + 2 * kind + half], sig[:, kind, half], ALU.mult).then_inc(prod, 1)

        @block.gpsimd
        def _(pool):
            pool.sem_inc(merged, PRIMED)
            with pool.Fori(0, KD) as m:
                for half in range(2):
                    pool.wait_ge(prod, PRIMED + 4 * m + 3 + half)
                    pool.tensor_tensor(mT[:, bass.ds(m, 1), half * 512:half * 512 + 512].rearrange("p a n -> p (a n)"),
                                       sig[:, 0, half], sig[:, 1, half], ALU.add).then_inc(merged, 1)


def out_norm(k, keep, mT, wo, x1, h2T, gates):
    nc, io = k.nc, k.io
    modT, ident, eps = keep["modT"], keep["ident"], keep["eps"]
    with ExitStack() as st:
        sem = lambda n: k.sem(st, "o_" + n)
        xt = k.sb(st, "xt_o", [P, 2, D])
        xn = k.sb(st, "xn_o", [P, 2, D])
        ss = k.sb(st, "ss_o", [P, 3, LT])
        ps = k.banks(st, "ps_o")
        x_in = [sem(f"x_in{j}") for j in range(2)]
        w_in = [sem(f"w_in{j}") for j in range(2)]
        g_in = sem("g_in")
        mm, x1_ok, sq_ok, rs_ok, xn_ok, turned, ev_a, ev_v, chain_v, chain_a = (
            sem(n) for n in ("mm", "x1_ok", "sq_ok", "rs_ok", "xn_ok", "turned", "ev_a", "ev_v", "chain_v", "chain_a"))
        block = st.enter_context(nc.Block())

        @block.sync
        def _(sp):
            w = io["w_late"][0:D].rearrange("(k p) n -> p k n", p=P)
            for half in range(2):
                sp.dma_start(wo[:, :, half * 512:half * 512 + 512], w[:, :, half * 512:half * 512 + 512]).then_inc(w_in[half], 16)
            sp.dma_start(gates[:], io["gate_rows"]).then_inc(g_in, 16)
            for t in range(LT):
                if t >= 2:
                    sp.wait_ge(x1_ok, t - 1)
                sp.dma_start(xt[:, t % 2], io["x"][0, t * P:(t + 1) * P]).then_inc(x_in[t % 2], 16)

        @block.tensor
        def _(pe):
            def turn(t):
                pe.wait_ge(xn_ok, t + 1)
                if t >= 2:
                    pe.wait_ge(ev_a, t - 1)
                    pe.wait_ge(ev_v, t - 1)
                for h in range(2):
                    for j in range(4):
                        ins = pe.transpose(ps[:, 4 + 2 * (t % 2) + h, j * P:(j + 1) * P],
                                           xn[:, t % 2, (4 * h + j) * P:(4 * h + j + 1) * P], ident[:])
                    ins.then_inc(turned, 1)
            for t in range(LT):
                if t >= 2:
                    pe.wait_ge(x1_ok, t - 1)
                for half in range(2):
                    pe.wait_ge(w_in[half], 16)
                    for kk in range(KD):
                        ins = pe.matmul(ps[:, 2 * (t % 2) + half], mT[:, kk, t * P:(t + 1) * P], wo[:, kk, half * 512:half * 512 + 512],
                                        start=kk == 0, stop=kk == KD - 1)
                ins.then_inc(mm, 1)
                if t >= 1:
                    turn(t - 1)
            turn(LT - 1)

        @block.vector
        def _(dve):
            step = Chain(dve, chain_v)

            def evac(t):
                dve.wait_ge(turned, 2 * t + 1)
                for j in range(4):
                    ins = dve.tensor_scalar(h2T[:, j, t * P:(t + 1) * P], ps[:, 4 + 2 * (t % 2), j * P:(j + 1) * P],
                                            modT[:, 24 + j, 0:1], modT[:, 16 + j, 0:1], ALU.mult, ALU.add)
                ins.then_inc(ev_v, 1)
            dve.wait_ge(g_in, 16)
            for t in range(LT):
                dve.wait_ge(mm, t + 1)
                step(dve.tensor_tensor(x1[:, t], ps[:, 2 * (t % 2):2 * (t % 2) + 2].rearrange("p b n -> p (b n)"), gates[:, 0], ALU.mult))
                dve.wait_ge(x_in[t % 2], 16 * (t // 2 + 1))
                dve.tensor_tensor(x1[:, t], x1[:, t], xt[:, t % 2], ALU.add).then_inc(x1_ok, 1)
                dve.wait_ge(rs_ok, t + 1)
                if t >= 2:
                    dve.wait_ge(turned, 2 * t - 2)
                dve.tensor_scalar(xn[:, t % 2], x1[:, t], ss[:, 2, t:t + 1], None, ALU.mult).then_inc(xn_ok, 1)
                if t >= 1:
                    evac(t - 1)
            evac(LT - 1)

        @block.scalar
        def _(act):
            step = Chain(act, chain_a)

            def evac(t):
                act.wait_ge(turned, 2 * t + 2)
                for j in range(4):
                    ins = act.activation(h2T[:, 4 + j, t * P:(t + 1) * P], ps[:, 5 + 2 * (t % 2), j * P:(j + 1) * P],
                                         ACT.Identity, bias=modT[:, 20 + j, 0:1], scale=modT[:, 28 + j, 0:1])
                ins.then_inc(ev_a, 1)
            for t in range(LT):
                act.wait_ge(x1_ok, t + 1)
                if t >= 2:
                    act.wait_ge(turned, 2 * t - 2)
                step(act.activation(xn[:, t % 2], x1[:, t], ACT.Square, accum_out=ss[:, 0, t:t + 1]))
                step(act.activation(ss[:, 1, t:t + 1], ss[:, 0, t:t + 1], ACT.Ln, bias=eps[:], scale=1.0 / D))
                act.activation(ss[:, 2, t:t + 1], ss[:, 1, t:t + 1], ACT.Exp, scale=-0.5).then_inc(rs_ok, 1)
                if t >= 1:
                    evac(t - 1)
            evac(LT - 1)


SLICES = FF // D


def mlp(k, keep, x1, h2T, hid, w1, w2, gates):
    nc, io = k.nc, k.io
    J = 2 * KD
    with ExitStack() as st:
        sem = lambda n: k.sem(st, "f_" + n)
        rl = k.sb(st, "rl", [P, 2, 512])
        tmp = k.sb(st, "tmp_f", [P, 2, 512])
        ps = k.banks(st, "ps_f")
        w1_in = [sem(f"w1_in{j}") for j in range(KD)]
        w2_in = [sem(f"w2_in{j}") for j in range(KD)]
        mm1, relu, sq_ok, mm2, gated, acc, out_ok = (sem(n) for n in ("mm1", "relu", "sq_ok", "mm2", "gated", "acc", "out_ok"))
        block = st.enter_context(nc.Block())
        v1 = io["w_mlp1"][0].rearrange("(k p) n -> p k n", p=P)
        v2 = io["w_mlp2"][0].rearrange("(k p) n -> p k n", p=P)

        @block.sync
        def _(sp):
            def loads(s, first):
                for j in range(KD):
                    if not first:
                        sp.wait_ge(mm1, J * s - J + 2 * j + 2)
                    sp.dma_start(w1[:, j], v1[:, :, bass.ds(s * D + j * P, P)]).then_inc(w1_in[j], 16)
                for j in range(KD):
                    if not first:
                        sp.wait_ge(mm2, J * s)
                    sp.dma_start(w2[:, j], v2[:, bass.ds(s * KD + j, 1)].rearrange("p a n -> p (a n)")).then_inc(w2_in[j], 16)
            loads(0, True)
            with sp.Fori(0, SLICES - 1) as s:
                loads(s + 1, False)
            for t in range(LT):
                sp.wait_ge(acc, J * (SLICES - 1) + 2 * t + 2)
                sp.dma_start(io["out"][0, t * P:(t + 1) * P], x1[:, t]).then_inc(out_ok, 16)
            sp.wait_ge(out_ok, 16 * LT)

        @block.tensor
        def _(pe):
            with pe.Fori(0, SLICES) as s:
                for j in range(KD):
                    pe.wait_ge(w1_in[j], 16 * s + 16)
                    for half in range(2):
                        n = 2 * j + half
                        pe.wait_ge(relu, J * s + max(n - 3, 0))
                        for kk in range(KD):
                            ins = pe.matmul(ps[:, n % 4], w1[:, j, kk], h2T[:, kk, half * 512:half * 512 + 512],
                                            start=kk == 0, stop=kk == KD - 1)
                        ins.then_inc(mm1, 1)
                for n in range(J):
                    t, half = n // 2, n % 2
                    pe.wait_ge(gated, J * s + max(n - 3, 0))
                    if n == 0:
                        pe.wait_ge(sq_ok, J * s + J)
                    for kk in range(KD):
                        if n == 0:
                            pe.wait_ge(w2_in[kk], 16 * s + 16)
                        ins = pe.matmul(ps[:, 4 + n % 4], hid[:, kk, t * P:(t + 1) * P], w2[:, kk, half * 512:half * 512 + 512],
                                        start=kk == 0, stop=kk == KD - 1)
                    ins.then_inc(mm2, 1)

        @block.scalar
        def _(act):
            with act.Fori(0, SLICES) as s:
                for n in range(J):
                    act.wait_ge(mm1, J * s + n + 1)
                    act.wait_ge(sq_ok, J * s + max(n - 1, 0))
                    act.activation(rl[:, n % 2], ps[:, n % 4], ACT.Relu).then_inc(relu, 1)

        @block.vector
        def _(dve):
            with dve.Fori(0, SLICES) as s:
                for n in range(J):
                    dve.wait_ge(relu, J * s + n + 1)
                    dve.tensor_tensor(hid[:, n // 2, (n % 2) * 512:(n % 2) * 512 + 512], rl[:, n % 2], rl[:, n % 2], ALU.mult).then_inc(sq_ok, 1)
                for n in range(J):
                    dve.wait_ge(mm2, J * s + n + 1)
                    dve.wait_ge(acc, J * s + max(n - 1, 0))
                    dve.tensor_tensor(tmp[:, n % 2], ps[:, 4 + n % 4], gates[:, 1, (n % 2) * 512:(n % 2) * 512 + 512], ALU.mult).then_inc(gated, 1)

        @block.gpsimd
        def _(pool):
            with pool.Fori(0, SLICES) as s:
                for n in range(J):
                    pool.wait_ge(gated, J * s + n + 1)
                    o = x1[:, n // 2, (n % 2) * 512:(n % 2) * 512 + 512]
                    pool.tensor_tensor(o, o, tmp[:, n % 2], ALU.add).then_inc(acc, 1)


def build(nc, io, upto=99):
    k = Ctx(nc, io)
    with ExitStack() as root:
        keep = {"ident": k.sb(root, "ident", [P, P]), "masks": k.sb(root, "masks", [P, 4, P]),
                "modT": k.sb(root, "modT", [P, 32, 2]), "eps": k.sb(root, "eps", [P, 1])}
        modulation(k, keep)
        with ExitStack() as st_h:
            hT = k.sb(st_h, "hT", [P, KD, NTOK])
            norm_in(k, keep, hT)
            if upto == 1:
                return dump(k, [("dbg_hT", hT[:].rearrange("p k n -> p (k n)"))])
            if upto != 4:
              with ExitStack() as st:
                tab = k.sb(st, "tab", [P, GROUPS, T_ALL])
                ssd_tables(k, keep, hT, tab)
                if upto == 2:
                    return dump(k, [("dbg_tab", tab[:].rearrange("p g n -> p (g n)"))])
                ssd_groups(k, keep, hT, tab)
                if upto == 3:
                    return dump(k, [("dbg_uT", io["uT"])])

            attT = k.sb(st_h, "attT", [P, PAIRS, NLAT])
            with ExitStack() as st:
                cqT = k.sb(st, "cqT", [P, 2, NLAT])
                ckvT = k.sb(st, "ckvT", [P, NTOK])
                kst = k.sb(st, "kst", [P, NT, 2, QKD])
                compress(k, keep, hT, cqT, ckvT, kst)
                attention(k, keep, hT, cqT, ckvT, kst, attT)
            if upto == 4:
                return dump(k, [("dbg_attT", attT[:].rearrange("p k n -> p (k n)"))])

            uT = k.sb(st_h, "uT", [P, 2 * GROUPS, NLAT])
            mT = k.sb(st_h, "mT", [P, KD, NLAT])
            gates = k.sb(st_h, "gate_rows_sb", [P, 2, D])
            merge(k, keep, hT, attT, uT, mT)
            h2T, x1, w2 = hT[:, :, 0:NLAT], attT, uT[:, 0:KD]
            w1 = uT[:, KD:].rearrange("p j (k n) -> p j k n", n=P)
            out_norm(k, keep, mT, w2, x1, h2T, gates)
            mlp(k, keep, x1, h2T, mT, w1, w2, gates)


def dump(k, items):
    with ExitStack() as st:
        out = k.sem(st, "dbg_out")
        block = st.enter_context(k.nc.Block())

        @block.sync
        def _(sp):
            for n, (name, src) in enumerate(items):
                sp.dma_start(k.io[name], src).then_inc(out, 16)
                sp.wait_ge(out, 16 * (n + 1))


def _constants():
    a = np.arange(P)
    row, col = a[:, None], a[None, :]
    masks = np.stack([row <= col, row >= col, row < col, row > col], 1).astype(np.float32)
    pos = np.arange(NLAT)
    pairs = ROPE // 4
    freqs = np.float32(10000.0) ** (-np.arange(pairs, dtype=np.float32) / np.float32(pairs))
    ang = np.stack([pos // 64, pos % 64], -1).astype(np.float32)[..., None] * freqs
    cos, sin = np.cos(ang), np.sin(ang)
    cos2 = np.stack([cos, cos], 2).reshape(LT, P, ROPE)
    sin2 = np.stack([-sin, sin], 2).reshape(LT, P, ROPE)
    rope = np.stack([cos2, sin2], 0).transpose(2, 0, 1, 3)
    return {"ident": np.eye(P, dtype=np.float32), "masks": masks, "rope": np.ascontiguousarray(rope, np.float32)}


def _layouts(x):
    def cols(a):
        return a.reshape(-1, P).T
    cw = x["conv_w"][0].T.reshape(4 * GROUPS, P, TAPS)
    cb = x["conv_b"][0].reshape(4 * GROUPS, P, 1)
    conv = np.concatenate([cw, cb], -1)
    tiles = np.stack([np.stack([conv[2 * g], conv[2 * g + 1], conv[16 + g], conv[24 + g]], 0) for g in range(GROUPS)], 0)
    return {
        "cvec": np.stack([cols(x["c"][0]), cols(x["c_ctx"])], -1),
        "b_modT": cols(x["b_mod"][0]), "norm1": cols(x["norm1_g"][0]), "norm2": cols(x["norm2_g"][0]),
        "q_gain": cols(x["q_a_g"][0]), "kv_gain": cols(x["kv_a_g"][0]),
        "conv": tiles.transpose(2, 0, 1, 3),
        "ssm_gain": x["ssm_norm_g"][0].reshape(GROUPS, 2, P).transpose(2, 0, 1),
        "w_late": np.concatenate([x["w_out"][0], x["w_proj_a"][0], x["w_proj_b"][0]], 0),
        "qk_gain": np.stack([x["qk_q_g"][0], x["qk_k_g"][0]], -1),
    }


_RAW = ["x", "ctx", "w_mod", "b_mod", "w_in", "w_uq", "w_ukv", "qk_q_g", "qk_k_g", "dt_bias", "a_log", "d_skip",
        "w_mlp1", "w_mlp2"]


def program(inputs, nc, mybir_, extra=()):
    x = {n: np.asarray(a) for n, a in inputs.items()}
    given = {n: x[n] for n in _RAW} | _layouts(x) | _constants()
    arrays, io = {}, {}
    for name, a in given.items():
        arrays[f"in_{name}"] = np.ascontiguousarray(a)
        io[name] = nc.dram_tensor(f"in_{name}", a.shape, F32, kind="ExternalInput").ap()
    io["out"] = nc.dram_tensor("out_0", (1, NLAT, D), F32, kind="ExternalOutput").ap()
    io["gate_rows"] = nc.dram_tensor("gate_rows", (P, 2, D), F32, kind="Internal").ap()
    io["uT"] = nc.dram_tensor("uT_rows", (2 * GROUPS, P, NLAT), F32, kind="Internal").ap()
    for name, shape in extra:
        io[name] = nc.dram_tensor(name, shape, F32, kind="ExternalOutput").ap()
    return arrays, io


def kernel(**inputs):
    import concourse.bacc as _bacc
    from concourse import mybir as _mybir
    from concourse.bass_utils import run_bass_kernel_spmd as _run

    nc = _bacc.Bacc("TRN2", target_bir_lowering=False, num_devices=1)
    arrays, io = program(inputs, nc, _mybir)
    build(nc, io)
    r = _run(nc, [arrays], core_ids=[0])
    return r.results[0]["out_0"]
```

```python
from contextlib import ExitStack

import numpy as np

import concourse.bass as bass
from concourse import mybir

F32 = mybir.dt.float32
F32R = mybir.dt.float32r
ALU = mybir.AluOpType
ACT = mybir.ActivationFunctionType
AX_X = mybir.AxisListType.X
PRIMED = 1

P = 128
D = 1024
KD = D // P
NLAT, NCTX = 1024, 256
NTOK = NLAT + NCTX
LT, CT = NLAT // P, NCTX // P
NT = LT + CT
HEADS, NOPE, ROPE, VD = 16, 64, 32, 64
QKD = NOPE + ROPE
PAIRS = HEADS // 2
QL, KVL = 256, 128
DI = 2 * D
SH, GROUPS, DS = 32, 8, 128
R = SH // GROUPS
HP = DI // SH
GC = DI // GROUPS
TAPS = 5
PAD = TAPS // 2
FF = 4 * D
EPS = 1e-6
SCALE = float(QKD) ** -0.5
COL_CQ, COL_KR = 0, QL + KVL
COL_Z = COL_KR + ROPE
COL_X = COL_Z + DI
COL_B = COL_X + DI
COL_C = COL_B + GROUPS * DS
COL_DT = COL_C + GROUPS * DS
COL_GA = COL_DT + 2 * SH
COL_GB = COL_GA + D
NC_SMALL = COL_Z
UP, LOW, SUP, SLOW = range(4)


def bcast(ap, *shape):
    return ap.to_broadcast([ap.shape[0], *shape])


class Count:

    def __init__(self, sem, step=1, primed=0):
        self.sem, self.step, self.base, self.n = sem, step, primed, 0

    def loop(self, i, per):
        self.entry, self.per = self.base + self.n * self.step, per
        self.base, self.n = self.entry + i * (per * self.step), 0

    def leave(self, turns):
        assert self.n == self.per, (self.sem, self.n, self.per)
        self.base, self.n = self.entry + turns * self.per * self.step, 0

    def add(self, k=1):
        self.n += k
        return self.value()

    def value(self, back=0):
        return self.base + (self.n - back) * self.step

    def raised(self, ins):
        ins.then_inc(self.sem, self.step)
        return self.add()


class Chain(Count):

    def __init__(self, eng, sem):
        super().__init__(sem)
        self.eng = eng

    def __call__(self, ins):
        self.eng.wait_ge(self.sem, self.raised(ins))


class Ctx:

    def __init__(self, nc, io):
        self.nc, self.io = nc, io
        self.sems = []

    def sb(self, st, name, shape, dt=F32):
        return st.enter_context(self.nc.sbuf_tensor(name, shape, dt))

    def banks(self, st, name):
        return st.enter_context(self.nc.psum_tensor(name, [P, 8, 512], F32))

    def sem(self, st, name):
        self.sems.append(self.nc.alloc_semaphore(name=name))
        return self.sems[-1]

    def forget(self):
        self.nc.clear_and_free_semaphores(self.sems)
        self.nc.all_engine_barrier()
        self.sems = []


def modulation(k, keep):
    nc, io = k.nc, k.io
    with ExitStack() as st:
        cT = k.sb(st, "cT", [P, KD, 2])
        wm = k.sb(st, "wm", [P, 4, KD, 512])
        bT = k.sb(st, "bT", [P, 2 * KD])
        n1 = k.sb(st, "n1", [P, KD])
        act_c, modT = keep["act_c"], keep["modT"]
        ps = k.banks(st, "ps_mod")
        c_in = k.sem(st, "m_c_in")
        par_in = k.sem(st, "m_par_in")
        w_in = [k.sem(st, f"m_w_in{s}") for s in range(4)]
        w_done = k.sem(st, "m_w_done")
        acted = k.sem(st, "m_acted")
        chain = k.sem(st, "m_chain")
        block = st.enter_context(nc.Block())
        w = io["w_mod"][0].rearrange("(k p) n -> p k n", p=P)

        @block.sync
        def _(sp):
            sp.dma_start(cT[:], io["cvec"]).then_inc(c_in, 16)
            for b in range(4):
                sp.dma_start(wm[:, b], w[:, :, b * 512:(b + 1) * 512]).then_inc(w_in[b], 16)

        @block.gpsimd
        def _(pool):
            n = 0
            for dst, src in ((bT[:], io["b_modT"][:, 0:2 * KD]), (n1[:], io["norm1"]),
                             (keep["ident"][:], io["ident"]), (keep["masks"][:], io["masks"])):
                pool.dma_start(dst, src).then_inc(par_in, 16)
                n += 16
            pool.wait_ge(par_in, n)

        @block.scalar
        def _(act):
            act.wait_ge(c_in, 16)
            act.activation(act_c[:], cT[:], ACT.Silu).then_inc(acted, 1)

        @block.tensor
        def _(pe):
            pe.wait_ge(acted, 1)
            for b in range(4):
                pe.wait_ge(w_in[b], 16)
                for c in range(4):
                    o = ps[:, 0, (4 * b + c) * 2:(4 * b + c) * 2 + 2]
                    for kk in range(KD):
                        mm = pe.matmul(o, wm[:, b, kk, c * P:(c + 1) * P], act_c[:, kk], start=kk == 0, stop=kk == KD - 1)
                mm.then_inc(w_done, 1)

        @block.vector
        def _(dve):
            step = Chain(dve, chain)
            dve.wait_ge(par_in, 16 * 4)
            dve.wait_ge(w_done, 4)
            raw = ps[:, 0, 0:32].rearrange("p (c s) -> p c s", s=2)
            step(dve.tensor_tensor(modT[:, 0:16], raw, bcast(bT[:].unsqueeze(2), 16, 2), ALU.add))
            s = modT[:, 8:16]
            step(dve.tensor_scalar(s, s, 1.0, None, ALU.add))
            step(dve.tensor_tensor(s, s, bcast(n1[:].unsqueeze(2), KD, 2), ALU.mult))


RMS_GROUPS = ((0, 2), (2, 6), (6, NT))


def norm_in(k, keep, hT):
    nc, io = k.nc, k.io
    modT, ident, eps = keep["modT"], keep["ident"], keep["eps"]
    with ExitStack() as st:
        xt = k.sb(st, "xt", [P, NT, D])
        xn = k.sb(st, "xn", [P, 2, D])
        junk = k.sb(st, "junk", [P, 2, D])
        ss = k.sb(st, "ss", [P, 3, NT])
        ps = k.banks(st, "ps_norm")
        x_in = [k.sem(st, f"n_x_in{t}") for t in range(NT)]
        rs = k.sem(st, "n_rs")
        xn_ok = k.sem(st, "n_xn")
        turned = k.sem(st, "n_turned")
        ev_a, ev_v = k.sem(st, "n_ev_a"), k.sem(st, "n_ev_v")
        eps_ok = k.sem(st, "n_eps")
        h_out = k.sem(st, "n_h_out")
        chain = k.sem(st, "n_chain")
        block = st.enter_context(nc.Block())

        @block.sync
        def _(sp):
            for t in range(NT):
                src = io["ctx"][0, t * P:(t + 1) * P] if t < CT else io["x"][0, (t - CT) * P:(t - CT + 1) * P]
                sp.dma_start(xt[:, t], src).then_inc(x_in[t], 16)
            for t in range(NT):
                sp.wait_ge(ev_a, t + 1)
                sp.wait_ge(ev_v, t + 1)
                sp.dma_start(io["hT"][:, :, t * P:(t + 1) * P].rearrange("k p n -> p k n"), hT[:, :, t * P:(t + 1) * P]).then_inc(h_out, 16)
            sp.wait_ge(h_out, 16 * NT)

        @block.scalar
        def _(act):
            act.wait_ge(eps_ok, 1)
            step = Chain(act, chain)

            def rstd(g):
                a, b = RMS_GROUPS[g]
                for t in range(a, b):
                    act.wait_ge(x_in[t], 16)
                    ins = act.activation(junk[:, t % 2], xt[:, t], ACT.Square, accum_out=ss[:, 0, t:t + 1])
                    step(ins)
                step(act.activation(ss[:, 1, a:b], ss[:, 0, a:b], ACT.Ln, bias=eps[:], scale=1.0 / D))
                act.activation(ss[:, 2, a:b], ss[:, 1, a:b], ACT.Exp, scale=-0.5).then_inc(rs, 1)

            def evac(t):
                act.wait_ge(turned, 2 * t + 2)
                s = 1 if t < CT else 0
                for j in range(4):
                    ins = act.activation(hT[:, 4 + j, t * P:(t + 1) * P], ps[:, 2 * (t % 2) + 1, j * P:(j + 1) * P],
                                         ACT.Identity, bias=modT[:, 4 + j, s:s + 1], scale=modT[:, 12 + j, s:s + 1])
                ins.then_inc(ev_a, 1)
            rstd(0)
            for g in range(len(RMS_GROUPS)):
                if g + 1 < len(RMS_GROUPS):
                    rstd(g + 1)
                for t in range(*RMS_GROUPS[g]):
                    evac(t)

        def evac(dve, t):
            dve.wait_ge(turned, 2 * t + 1)
            s = 1 if t < CT else 0
            for j in range(4):
                ins = dve.tensor_scalar(hT[:, j, t * P:(t + 1) * P], ps[:, 2 * (t % 2), j * P:(j + 1) * P],
                                        modT[:, 8 + j, s:s + 1], modT[:, j, s:s + 1], ALU.mult, ALU.add)
            ins.then_inc(ev_v, 1)

        @block.vector
        def _(dve):
            dve.memset(eps[:], EPS).then_inc(eps_ok, 1)
            for t in range(NT):
                dve.wait_ge(rs, 1 + sum(t >= b for _, b in RMS_GROUPS))
                if t >= 2:
                    dve.wait_ge(turned, 2 * t - 2)
                dve.tensor_scalar(xn[:, t % 2], xt[:, t], ss[:, 2, t:t + 1], None, ALU.mult).then_inc(xn_ok, 1)
                if t >= 1:
                    evac(dve, t - 1)
            evac(dve, NT - 1)

        @block.tensor
        def _(pe):
            for t in range(NT):
                pe.wait_ge(xn_ok, t + 1)
                if t >= 2:
                    pe.wait_ge(ev_a, t - 1)
                    pe.wait_ge(ev_v, t - 1)
                for h in range(2):
                    for j in range(4):
                        ins = pe.transpose(ps[:, 2 * (t % 2) + h, j * P:(j + 1) * P],
                                           xn[:, t % 2, (4 * h + j) * P:(4 * h + j + 1) * P], ident[:])
                    ins.then_inc(turned, 1)


T_DT, T_WEND, T_EA, T_CD, T_DA = (i * NT * 2 * R for i in range(5))
T_SKIP = 5 * NT * 2 * R
T_ALL = T_SKIP + R


def step_chunk(d, s):
    if d == 0:
        return s
    return CT - 1 - s if s < CT else NT - 1 - (s - CT)


def ssd_tables(k, keep, hT):
    nc, io = k.nc, k.io
    masks = keep["masks"]
    N = NT * 2 * SH
    with ExitStack() as st:
        wdt = k.sb(st, "wdt", [P, KD, P])
        bias = k.sb(st, "bias", [P, 2 * SH])
        alog = k.sb(st, "alog", [P, 2 * SH])
        skip = k.sb(st, "skip", [P, 2, SH])
        nega = k.sb(st, "nega", [P, 2 * SH])
        v, m, e, u, l, dd, dA = (k.sb(st, f"sp_{n}", [P, N]) for n in "vmeuldA")
        ones = k.sb(st, "ones", [P, P])
        tab = k.sb(st, "tab_sb", [P, GROUPS, T_ALL])
        ps = k.banks(st, "ps_dt")
        tab_ok, tab_out = k.sem(st, "t_tab_ok"), k.sem(st, "t_tab_out")
        t_in, mm, chain, dve_ok, act_ok, dec = (k.sem(st, "t_" + n) for n in ("in", "mm", "chain", "dve", "act", "dec"))
        block = st.enter_context(nc.Block())

        def kind(col, d):
            g = tab[:, :, col:col + NT * 2 * R].rearrange("p g (c d r) -> p g c d r", d=2, r=R)[:, :, :, d]
            return g.rearrange("p g c r -> p c g r")

        def raw(t, d):
            return t[:].rearrange("p (c d h) -> p c d h", c=NT, d=2)[:, :, d]

        def raw4(t, d):
            return t[:].rearrange("p (c d g r) -> p c d g r", c=NT, d=2, r=R)[:, :, d]

        @block.sync
        def _(sp):
            sp.dma_start(wdt[:], io["w_in"][0].rearrange("(k p) n -> p k n", p=P)[:, :, COL_GA - P:COL_GA]).then_inc(t_in, 16)
            sp.dma_start(bias[:], io["dt_bias"][0].rearrange("d h -> (d h)").partition_broadcast(P)).then_inc(t_in, 16)
            sp.dma_start(alog[:], io["a_log"][0].rearrange("d h -> (d h)").partition_broadcast(P)).then_inc(t_in, 16)
            sp.dma_start(skip[:], io["d_skip"][0].partition_broadcast(P)).then_inc(t_in, 16)
            sp.wait_ge(tab_ok, 1)
            sp.wait_ge(act_ok, 8)
            sp.dma_start(io["tab"], tab[:]).then_inc(tab_out, 16)
            sp.wait_ge(tab_out, 16)

        @block.tensor
        def _(pe):
            pe.wait_ge(t_in, 64)
            for t in range(NT):
                o = ps[:, t // 4, (t % 4) * P:(t % 4 + 1) * P]
                for kk in range(KD):
                    ins = pe.matmul(o, hT[:, kk, t * P:(t + 1) * P], wdt[:, kk], start=kk == 0, stop=kk == KD - 1)
            ins.then_inc(mm, 1)
            pe.wait_ge(dve_ok, 2)
            for b, (w, d) in enumerate(((SLOW, 0), (SUP, 1), (UP, 0), (LOW, 1), (None, 0), (None, 1))):
                pe.matmul(ps[:, 2 + b, 0:NT * SH], ones[:] if w is None else masks[:, w], raw(dA, d),
                          start=True, stop=True).then_inc(dec, 1)

        @block.scalar
        def _(act):
            act.wait_ge(t_in, 64)
            act.activation(nega[:], alog[:], ACT.Exp).then_inc(act_ok, 1)
            act.wait_ge(dve_ok, 1)
            act.activation(e[:], e[:], ACT.Exp).then_inc(act_ok, 1)
            act.wait_ge(act_ok, 2)
            act.activation(l[:], e[:], ACT.Ln, bias=1.0).then_inc(act_ok, 1)
            for b, (col, d) in enumerate(((T_WEND, 0), (T_WEND, 1), (T_EA, 0), (T_EA, 1))):
                act.wait_ge(dec, b + 1)
                act.activation(kind(col, d), ps[:, 2 + b, 0:NT * SH].rearrange("p (c g r) -> p c g r", c=NT, r=R),
                               ACT.Exp).then_inc(act_ok, 1)
            for d in range(2):
                act.wait_ge(dec, 5 + d)
                for s in range(NT):
                    c = step_chunk(d, s)
                    ins = act.activation(kind(T_CD, d)[:, s], ps[:, 6 + d, c * SH:(c + 1) * SH].rearrange("p (g r) -> p g r", r=R), ACT.Exp)
            ins.then_inc(act_ok, 1)

        @block.vector
        def _(dve):
            step = Chain(dve, chain)
            step(dve.memset(ones[:], 1.0))
            dve.wait_ge(mm, 1)
            for b, n in ((0, 4), (1, 4), (2, NT - 8)):
                step(dve.tensor_tensor(v[:, b * 256:b * 256 + n * 64].rearrange("p (c h) -> p c h", h=64),
                                       ps[:, b, 0:n * P].rearrange("p (c h) -> p c h", h=P)[:, :, P - 64:],
                                       bcast(bias[:].unsqueeze(1), n, 64), ALU.add))
            step(dve.tensor_scalar(m[:], v[:], 0.0, None, ALU.max))
            step(dve.tensor_scalar(e[:], v[:], -1.0, None, ALU.mult))
            dve.tensor_tensor(e[:], e[:], v[:], ALU.min).then_inc(dve_ok, 1)
            dve.wait_ge(act_ok, 3)
            step(dve.tensor_scalar(u[:], e[:], 1.0, -1.0, ALU.add, ALU.add))
            step(dve.tensor_scalar(dd[:], u[:], 0.0, None, ALU.is_equal))
            step(dve.tensor_tensor(u[:], u[:], dd[:], ALU.add))
            step(dve.tensor_tensor(l[:], l[:], dd[:], ALU.add))
            step(dve.tensor_tensor(l[:], l[:], e[:], ALU.mult))
            step(dve.reciprocal(u[:], u[:]))
            step(dve.tensor_tensor(l[:], l[:], u[:], ALU.mult))
            step(dve.tensor_tensor(m[:], l[:], m[:], ALU.add))
            step(dve.tensor_scalar(nega[:], nega[:], -1.0, None, ALU.mult))
            dve.tensor_tensor(dA[:].rearrange("p (c h) -> p c h", h=64), m[:].rearrange("p (c h) -> p c h", h=64),
                              bcast(nega[:].unsqueeze(1), NT, 64), ALU.mult).then_inc(dve_ok, 1)
            dve.wait_ge(dve_ok, 2)
            for d in range(2):
                dve.tensor_copy(kind(T_DT, d), raw4(m, d))
                dve.tensor_copy(kind(T_DA, d), raw4(dA, d))
            dve.tensor_tensor(tab[:, :, T_SKIP:T_ALL], skip[:, 0].rearrange("p (g r) -> p g r", r=R),
                              skip[:, 1].rearrange("p (g r) -> p g r", r=R), ALU.add)
            dve.wait_ge(act_ok, 7)
            for d in range(2):
                ins = dve.tensor_tensor(kind(T_WEND, d), kind(T_WEND, d), raw4(m, d), ALU.mult)
            ins.then_inc(tab_ok, 1)


XPAD = NCTX + PAD
CONVN = NCTX + PAD + NLAT
SEGS = ((0, 0, NCTX), (XPAD, NCTX, 512), (XPAD + 512, NCTX + 512, 512))
TURN_ORDER = [0, 1] + [c for s in range(2, 2 + LT // 2) for c in (s, NT - 1 + CT - s)]
STEPS = NT - 1
RING_P = 4 * 3 - 1
RING_T = RING_P + NT
RING = RING_T + LT // 2


def tok_col(c):
    return c * P if c < CT else XPAD + (c - CT) * P


def ssd_groups(k, keep, hH, hL):
    nc, io = k.nc, k.io
    masks, ident, eps = keep["masks"], keep["ident"], keep["eps"]
    w = io["w_in"][0].rearrange("(k p) n -> p k n", p=P)
    with ExitStack() as st:
        sb = lambda n, s: k.sb(st, n, s)
        sem = lambda n: k.sem(st, "s_" + n)
        raw = sb("raw_s", [P, 2, D])
        wr = [k.sb(st, n, [P, KD, 2, P], F32R) for n in ("wrH", "wrL")]
        conv = sb("conv", [P, GROUPS, 4, TAPS + 1])
        gains = sb("gains", [P, GROUPS, 2])
        cg = sb("cg", [P, 4, TAPS + 1])
        tg = sb("tg", [P, T_ALL])
        sg = sb("sg", [P, 2])
        work = sb("work", [P, 2 * (CONVN + 2 * PAD) + 2 * CONVN])
        xb = sb("xb", [P, 4, CONVN])
        tk = sb("tk", [P, NT, GC + DS])
        u = sb("u", [P, LT, GC])
        H = sb("H", [P, STEPS, 2 * GC])
        cbm = sb("cbm", [P, 2, P])
        xd = sb("xd", [P, GC])
        ss = sb("ss_u", [P, 3, LT])
        uo = sb("uo", [P, 2, 512])
        junk = sb("junk_u", [P, GC])
        ps = k.banks(st, "ps_ssd")

        def shares(ap, start, shape):
            n = int(np.prod(shape))
            names = "abc"[:len(shape)]
            return ap[:, start:start + n].rearrange(f"p ({' '.join(names)}) -> p {' '.join(names)}", **dict(zip(names[1:], shape[1:])))

        everything = work[:]
        pre = shares(everything, 0, (2, CONVN + 2 * PAD))
        cv = shares(everything, 2 * (CONVN + 2 * PAD), (2, CONVN))
        sr = shares(everything, 0, (2, 2, R * P))
        E = shares(everything, 4 * R * P, (2, R * P))
        EC = shares(everything, 6 * R * P, (2, 2, R * P))
        xw = shares(everything, 4 * R * P, (2, 2, GC))
        turned_xs = xb[:, 0:2].rearrange("p a n -> p (a n)")
        dtx = shares(turned_xs, 0, (2, 2, GC))
        t1 = shares(turned_xs, 4 * GC, (2, 2, GC))
        raw_in = [sem(f"raw_in{j}") for j in range(2)]
        whi_ok, pro_ok, itemA_ok, itemB_ok = sem("whi_ok"), sem("pro_ok"), sem("itemA_ok"), sem("itemB_ok")
        tab_in, tg_in = sem("tab_in"), sem("tg_in")
        ring_mm, ring_ev = sem("ring_mm"), sem("ring_ev")
        conv_ok, xb_ok = sem("conv_ok"), sem("xb_ok")
        xw_ok, st_mm, scanned = sem("xw_ok"), sem("st_mm"), sem("scanned")
        sr_ok, seg_mm, e_ok = sem("sr_ok"), sem("seg_mm"), sem("e_ok")
        cb_mm, cbm_ok, ec_ok = sem("cb_mm"), sem("cbm_ok"), sem("ec_ok")
        yo_mm, t1_ok, dtx_ok, y_mm = sem("yo_mm"), sem("t1_ok"), sem("dtx_ok"), sem("y_mm")
        s2_ok, u_ok, sq_ok, rs_ok, un_ok = sem("s2_ok"), sem("u_ok"), sem("sq_ok"), sem("rs_ok"), sem("un_ok")
        fin_mm, fin_ev, srb_ok = sem("fin_mm"), sem("fin_ev"), sem("srb_ok")
        pads, chain_v, chain_p, chain_a = sem("pads"), sem("chain_v"), sem("chain_p"), sem("chain_a")
        uo_out = [sem(f"uo_out{j}") for j in range(2)]
        block = st.enter_context(nc.Block())

        START = [("h", 0), ("h", 1), ("w", 0), ("w", 1)] + [("h", t) for t in range(2, NT)]
        PARTS = ((0, 0), (1, 0), (0, 1))
        h = (hH, hL)

        def start_parts(n):
            kind, t = START[n]
            at = raw[:, n % 2].rearrange("p (k n) -> p k n", n=P)
            if kind == "h":
                return at, hH[:, :, t * P:(t + 1) * P], hL[:, :, t * P:(t + 1) * P]
            return at, wr[0][:, :, t], wr[1][:, :, t]

        def item_parts(i):
            return raw[:, i % 2].rearrange("p (k n) -> p k n", n=P), wr[0][:, :, i % 2], wr[1][:, :, i % 2]

        def tgk(col, c, d):
            o = col + (c * 2 + d) * R
            return tg[:, o:o + R]

        def y_cols(ap):
            return ap.rearrange("p (a q x) -> p a q x", a=R // 2, x=HP)[:, :, 0:4:3]

        def per_head(ap, n=R):
            return ap.rearrange("p (r x) -> p r x", r=n)

        @block.sync
        def _(sp):
            sp.dma_start(conv[:], io["conv"]).then_inc(tab_in, 16)
            sp.dma_start(gains[:], io["ssm_gain"]).then_inc(tab_in, 16)

            def load(g, i):
                col = (COL_X + g * GC, COL_X + P + g * GC, COL_B + g * DS, COL_C + g * DS, COL_Z + g * GC, COL_Z + P + g * GC)[i]
                sp.dma_start(raw[:, i % 2].rearrange("p (k n) -> p k n", n=P), w[:, :, bass.ds(col, P)]).then_inc(raw_in[i % 2], 16)

            def loads(g, first):
                if not first:
                    for i in range(2):
                        sp.wait_ge(itemB_ok, 4 * g - 1 + i)
                        load(g, i)
                    sp.wait_ge(u_ok, PRIMED + LT * g)
                sp.dma_start(tg[:], io["tab"][:, bass.ds(g, 1)].rearrange("p a n -> p (a n)")).then_inc(tg_in, 16)
                for i in range(2, 6):
                    if i >= 4:
                        sp.wait_ge(itemB_ok, 4 * g + i - 3)
                    elif first:
                        sp.wait_ge(pro_ok, len(START))
                    else:
                        sp.wait_ge(itemA_ok, 2 * g - 1 + i - 2)
                    load(g, i)
            for n, (kind, t) in enumerate(START):
                if n >= 2:
                    sp.wait_ge(pro_ok, n - 1)
                if kind == "w":
                    load(0, t)
                else:
                    sp.dma_start(raw[:, n % 2].rearrange("p (k n) -> p k n", n=P),
                                 io["hT"][:, :, t * P:(t + 1) * P].rearrange("k p n -> p k n")).then_inc(raw_in[n % 2], 16)
            loads(0, True)
            with sp.Fori(1, GROUPS) as g:
                loads(g, False)

        @block.tensor
        def _(pe):
            for first in (ring_mm, st_mm, seg_mm, y_mm):
                pe.sem_inc(first, PRIMED)
            def group(g, first=False, last=False):
                n = 0

                def ring():
                    pe.wait_ge(ring_ev, PRIMED + RING * g + max(n - 1, 0))
                    return ps[:, n % 2]

                for ct in range(4):
                    if ct == 1 and not first:
                        turn_out(g - 1)
                    if ct >= 2:
                        pe.wait_ge(itemB_ok, 4 * g + ct - 1)
                    elif not first:
                        pe.wait_ge(itemA_ok, 2 * g - 1 + ct)
                    for _, tok, width in SEGS if ct < 3 else SEGS[1:]:
                        if first and ct == 0:
                            pe.wait_ge(pro_ok, {0: 3, NCTX: 8}.get(tok, len(START)))
                        o = ring()
                        for kk in range(KD):
                            for a, b in PARTS:
                                ins = pe.matmul(o[:, 0:width], wr[a][:, kk, ct % 2], h[b][:, kk, tok:tok + width],
                                                start=kk == 0 and (a, b) == PARTS[0], stop=kk == KD - 1 and (a, b) == PARTS[-1])
                        ins.then_inc(ring_mm, 1)
                        n += 1

                def gate(j, part, parts):
                    nonlocal n
                    if part == 0:
                        ring()
                    each = 2 * KD // parts
                    for i in range(part * each, (part + 1) * each):
                        half, kk = i // KD, i % KD
                        c0 = NCTX + (2 * j + half) * P
                        for a, b in PARTS:
                            ins = pe.matmul(ps[:, n % 2, half * GC:(half + 1) * GC], h[a][:, kk, c0:c0 + P],
                                            wr[b][:, kk].rearrange("p a n -> p (a n)"),
                                            start=kk == 0 and (a, b) == PARTS[0], stop=kk == KD - 1 and (a, b) == PARTS[-1])
                    if part == parts - 1:
                        ins.then_inc(ring_mm, 1)
                        n += 1
                pe.wait_ge(xb_ok, PRIMED + 4 * g + 3)
                for c in TURN_ORDER:
                    o = ring()
                    c0 = tok_col(c)
                    for ct in range(3):
                        ins = pe.transpose(o[:, ct * P:(ct + 1) * P], xb[:, ct, c0:c0 + P], ident[:])
                    ins.then_inc(ring_mm, 1)
                    n += 1
                pe.wait_ge(itemB_ok, 4 * g + 4)
                gate(0, 0, 1)
                gate(1, 0, 1)
                for s in range(STEPS):
                    pe.wait_ge(xw_ok, STEPS * g + s + 1)
                    if s < 2:
                        pe.wait_ge(e_ok, PRIMED + LT * g)
                    else:
                        pe.wait_ge(scanned, PRIMED + STEPS * g + s - 1)
                    for d in range(2):
                        ins = pe.matmul(ps[:, 2 + s % 2, d * GC:(d + 1) * GC], tk[:, step_chunk(d, s), GC:GC + DS],
                                        xw[:, s % 2, d], start=True, stop=True)
                    ins.then_inc(st_mm, 1)
                    if 1 <= s < 9:
                        gate(2 + (s - 1) // 4, (s - 1) % 4, 4)

                def heads(c):
                    c0 = tok_col(c + CT)
                    pe.wait_ge(sr_ok, LT * g + c + 1)
                    pe.wait_ge(srb_ok, LT * g + c + 1)
                    if c < 2:
                        pe.wait_ge(scanned, PRIMED + STEPS * g + STEPS)
                    else:
                        pe.wait_ge(e_ok, PRIMED + LT * g + c - 1)
                    pe.matmul(ps[:, 2 + c % 2], masks[:, SLOW], sr[:, c % 2, 0], start=True, stop=False)
                    pe.matmul(ps[:, 2 + c % 2], masks[:, SUP], sr[:, c % 2, 1], start=False, stop=True).then_inc(seg_mm, 1)
                    pe.wait_ge(cbm_ok, PRIMED + LT * g + c)
                    pe.matmul(ps[:, 4, 0:P], xb[:, 2, c0:c0 + P], xb[:, 3, c0:c0 + P],
                              start=True, stop=True).then_inc(cb_mm, 1)
                    pe.wait_ge(t1_ok, PRIMED + LT * g + c)
                    for d, s in ((0, c + CT - 1), (1, STEPS - 1 - c)):
                        ins = pe.matmul(ps[:, 5, d * GC:(d + 1) * GC], xb[:, 3, c0:c0 + P],
                                        H[:, s, d * GC:(d + 1) * GC], start=True, stop=True)
                    ins.then_inc(yo_mm, 1)

                pe.wait_ge(xb_ok, PRIMED + 4 * g + 4)
                pe.wait_ge(fin_ev, PRIMED + 4 * g)
                heads(0)
                for c in range(LT):
                    if c + 1 < LT:
                        heads(c + 1)
                    pe.wait_ge(ec_ok, PRIMED + LT * g + c + 1)
                    pe.wait_ge(dtx_ok, LT * g + c + 1)
                    pe.wait_ge(u_ok, PRIMED + LT * g + max(c - 1, 0))
                    for r in range(R):
                        for d in range(2):
                            ins = pe.matmul(ps[:, 6 + c % 2, r * P:(r + 1) * P], EC[:, c % 2, d, r * P:(r + 1) * P],
                                            dtx[:, c % 2, d, r // 2 * P:(r // 2 + 1) * P], start=d == 0, stop=d == 1)
                    ins.then_inc(y_mm, 1)
                assert n == RING

            def turn_out(g):
                for cc in range(2):
                    for half in range(2):
                        pe.wait_ge(un_ok, LT * g + 4 * half + 4)
                        for j in range(4):
                            ins = pe.transpose(ps[:, 4 + 2 * cc + half, j * P:(j + 1) * P], u[:, 4 * half + j, cc * P:(cc + 1) * P], ident[:])
                        ins.then_inc(fin_mm, 1)
            group(0, first=True)
            with pe.Fori(1, GROUPS) as g:
                group(g)
            turn_out(GROUPS - 1)

        @block.scalar
        def _(act):
            for first in (ring_ev, xb_ok, e_ok, sq_ok, fin_ev, *uo_out):
                act.sem_inc(first, PRIMED)
            act.wait_ge(pads, 1)
            act.wait_ge(tab_in, 32)

            def group(g, first=False, last=False):
                n = 0

                def job():
                    act.wait_ge(ring_mm, PRIMED + RING * g + n + 1)
                    return ps[:, n % 2]

                def to_rows(ct):
                    nonlocal n
                    act.wait_ge(conv_ok, PRIMED + 4 * g + max(ct - 1, 0))
                    for col, _, width in SEGS if ct < 3 else SEGS[1:]:
                        o = job()
                        act.activation(pre[:, ct % 2, PAD + col:PAD + col + width], o[:, 0:width], ACT.Copy).then_inc(ring_ev, 1)
                        n += 1

                def item(g, i):
                    act.wait_ge(raw_in[i % 2], 16 * (len(START) // 2 - 1 + 3 * g + i // 2 + 1))
                    act.wait_ge(ring_mm, PRIMED + RING * g + (3 * i - 3 if i < 5 else RING_P) if i >= 2 else PRIMED + RING * g)
                    src, hi, _ = item_parts(i)
                    act.activation(hi, src, ACT.Copy).then_inc(whi_ok, 1)

                def silu(ct):
                    act.wait_ge(conv_ok, PRIMED + 4 * g + ct + 1)
                    act.activation(xb[:, ct], cv[:, ct % 2], ACT.Silu).then_inc(xb_ok, 1)

                def gate(j):
                    nonlocal n
                    o = job()
                    act.activation(u[:, 2 * j:2 * j + 2], o.rearrange("p (t c) -> p t c", t=2), ACT.Silu).then_inc(ring_ev, 1)
                    n += 1

                to_rows(0)
                item(g, 2)
                if not first:
                    store(g - 1)
                to_rows(1)
                item(g, 3)
                silu(0)
                to_rows(2)
                item(g, 4)
                silu(1)
                to_rows(3)
                item(g, 5)
                silu(2)
                for c in TURN_ORDER:
                    o = job()
                    act.activation(tk[:, c], o[:, 0:GC + DS], ACT.Copy).then_inc(ring_ev, 1)
                    n += 1
                silu(3)
                gate(0)
                gate(1)

                gate(2)
                gate(3)
                if not last:
                    item(g + 1, 0)
                    item(g + 1, 1)
                act.wait_ge(tg_in, 16 * g + 16)
                act.wait_ge(st_mm, PRIMED + STEPS * g + STEPS)

                def masked(c):
                    act.wait_ge(seg_mm, PRIMED + LT * g + max(c - 1, 0))
                    for r in range(R):
                        o = T_DA + ((c + CT) * 2 + 1) * R + r
                        ins = act.activation(sr[:, c % 2, 1, r * P:(r + 1) * P], masks[:, LOW], ACT.Copy, scale=tg[:, o:o + 1])
                    ins.then_inc(srb_ok, 1)

                def decay(c):
                    act.wait_ge(seg_mm, PRIMED + LT * g + c + 1)
                    act.wait_ge(ec_ok, PRIMED + LT * g + max(c - 1, 0))
                    act.activation(E[:, c % 2], ps[:, 2 + c % 2], ACT.Exp).then_inc(e_ok, 1)

                masked(0)
                masked(1)
                for c in range(2):
                    decay(c)
                    masked(c + 2)
                for c in range(LT):
                    if c + 2 < LT:
                        decay(c + 2)
                    if c + 4 < LT:
                        masked(c + 4)
                    act.wait_ge(u_ok, PRIMED + LT * g + c + 1)
                    act.wait_ge(sq_ok, PRIMED + LT * g + c)
                    act.activation(junk[:], u[:, c], ACT.Square, accum_out=ss[:, 0, c:c + 1]).then_inc(sq_ok, 1)
                act.wait_ge(sq_ok, PRIMED + LT * g + LT)
                act.activation(ss[:, 1], ss[:, 0], ACT.Ln, bias=eps[:], scale=1.0 / GC).then_inc(chain_a, 1)
                act.wait_ge(chain_a, 2 * g + 1)
                act.activation(ss[:, 2], ss[:, 1], ACT.Exp, scale=-0.5).then_inc(rs_ok, 1)
                act.activation(sg[:], gains[:, bass.ds(g, 1)].rearrange("p a c -> p (a c)"), ACT.Copy).then_inc(chain_a, 1)
                act.wait_ge(chain_a, 2 * g + 2)
                assert n == RING

            def store(g):
                for cc in range(2):
                    for half in range(2):
                        j = 2 * cc + half
                        act.wait_ge(fin_mm, 4 * g + j + 1)
                        act.wait_ge(uo_out[j % 2], 32 * g + 16 * (j // 2) + PRIMED)
                        act.activation(uo[:, j % 2], ps[:, 4 + j], ACT.Copy, scale=sg[:, cc:cc + 1]).then_inc(fin_ev, 1)
                        act.wait_ge(fin_ev, PRIMED + 4 * g + j + 1)
                        act.dma_start(io["uT"][bass.ds(2 * g + cc, 1), :, half * 512:half * 512 + 512].rearrange("a p n -> p (a n)"),
                                      uo[:, j % 2]).then_inc(uo_out[j % 2], 16)
            for n in range(len(START)):
                act.wait_ge(raw_in[n % 2], 16 * (n // 2 + 1))
                src, hi, _ = start_parts(n)
                act.activation(hi, src, ACT.Copy).then_inc(whi_ok, 1)
            group(0, first=True)
            with act.Fori(1, GROUPS - 1) as g:
                group(g)
            group(GROUPS - 1, last=True)
            store(GROUPS - 1)
            for j in range(2):
                act.wait_ge(uo_out[j], 32 * GROUPS + PRIMED)

        @block.vector
        def _(dve):
            for first in (conv_ok, scanned, cbm_ok, ec_ok, t1_ok, u_ok):
                dve.sem_inc(first, PRIMED)
            step = Chain(dve, chain_v)
            dve.memset(cbm[:, 0, 0:1], 0.0).then_inc(pads, 1)
            dve.wait_ge(pads, 1)
            dve.wait_ge(tab_in, 32)
            for n in range(len(START)):
                dve.wait_ge(whi_ok, n + 1)
                src, hi, lo = start_parts(n)
                dve.tensor_tensor(lo, src, hi, ALU.subtract).then_inc(pro_ok, 1)

            def group(g, last=False):
                for b in range(2):
                    for c0 in (0, PAD + NCTX, CONVN + PAD):
                        step(dve.memset(pre[:, b, c0:c0 + PAD], 0.0))
                step(dve.tensor_copy(cg[:], conv[:, bass.ds(g, 1)].rearrange("p a c t -> p (a c) t")))
                for ct in range(4):
                    dve.wait_ge(ring_ev, PRIMED + RING * g + min(3 * ct + 3, RING_P))
                    dve.wait_ge(xb_ok, PRIMED + 4 * g + max(ct - 1, 0))
                    row, out = pre[:, ct % 2], cv[:, ct % 2]
                    step(dve.tensor_scalar(out, row[:, 0:CONVN], cg[:, ct, 0:1], cg[:, ct, TAPS:TAPS + 1], ALU.mult, ALU.add))
                    for tap in range(1, TAPS):
                        ins = dve.scalar_tensor_tensor(out, row[:, tap:tap + CONVN], cg[:, ct, tap:tap + 1], out, ALU.mult, ALU.add)
                        if tap < TAPS - 1:
                            step(ins)
                    ins.then_inc(conv_ok, 1)
                dve.wait_ge(tg_in, 16 * g + 16)
                for s in range(STEPS):
                    dve.wait_ge(st_mm, PRIMED + STEPS * g + s + 1)
                    new = ps[:, 2 + s % 2]
                    if s == 0:
                        dve.tensor_copy(H[:, 0], new).then_inc(scanned, 1)
                    else:
                        dve.wait_ge(scanned, PRIMED + STEPS * g + s)
                        step(dve.tensor_tensor(per_head(H[:, s], 2 * R), per_head(H[:, s - 1], 2 * R),
                                               bcast(tg[:, T_CD + s * 2 * R:T_CD + (s + 1) * 2 * R].unsqueeze(2), 2 * R, HP), ALU.mult))
                        dve.tensor_tensor(H[:, s], H[:, s], new, ALU.add).then_inc(scanned, 1)

                def gated(c):
                    dve.wait_ge(y_mm, PRIMED + LT * g + c + 1)
                    dve.wait_ge(s2_ok, PRIMED + LT * g + c + 1)
                    four = lambda a: a.rearrange("p (a q x) -> p a q x", a=R // 2, x=HP)
                    step(dve.tensor_tensor(four(t1[:, c % 2, 1]), y_cols(ps[:, 6 + c % 2]), four(t1[:, c % 2, 0]), ALU.add))
                    dve.tensor_tensor(u[:, c], u[:, c], t1[:, c % 2, 1], ALU.mult).then_inc(u_ok, 1)

                for c in range(LT):
                    dve.wait_ge(cb_mm, LT * g + c + 1)
                    dve.wait_ge(ec_ok, PRIMED + LT * g + c)
                    dve.tensor_tensor(cbm[:], bcast(ps[:, 4, 0:P].unsqueeze(1), 2, P), masks[:, UP:LOW + 1], ALU.mult).then_inc(cbm_ok, 1)
                    dve.wait_ge(cbm_ok, PRIMED + LT * g + c + 1)
                    dve.wait_ge(e_ok, PRIMED + LT * g + c + 1)
                    dve.wait_ge(y_mm, PRIMED + LT * g + max(c - 1, 0))
                    for d in range(2):
                        ins = dve.tensor_tensor(per_head(EC[:, c % 2, d]), per_head(E[:, c % 2]),
                                                bcast(cbm[:, d].unsqueeze(1), R, P), ALU.mult)
                    ins.then_inc(ec_ok, 1)
                    dve.wait_ge(yo_mm, LT * g + c + 1)
                    if c >= 2:
                        dve.wait_ge(u_ok, PRIMED + LT * g + c - 1)
                    o = T_EA + (c + CT) * 2 * R
                    dve.tensor_tensor(t1[:, c % 2].rearrange("p d (r x) -> p (d r) x", r=R), per_head(ps[:, 5], 2 * R),
                                      bcast(tg[:, o:o + 2 * R].unsqueeze(2), 2 * R, HP), ALU.mult).then_inc(t1_ok, 1)
                    if c >= 1:
                        gated(c - 1)
                    if not last and c in (3, 5):
                        i = (c - 3) // 2
                        dve.wait_ge(whi_ok, len(START) + 6 * g + 4 + i + 1)
                        src, hi, lo = item_parts(i)
                        dve.tensor_tensor(lo, src, hi, ALU.subtract).then_inc(itemA_ok, 1)
                gated(LT - 1)
                dve.wait_ge(rs_ok, g + 1)
                for c in range(LT):
                    dve.tensor_scalar(u[:, c], u[:, c], ss[:, 2, c:c + 1], None, ALU.mult).then_inc(un_ok, 1)
            with dve.Fori(0, GROUPS - 1) as g:
                step.loop(g, STEPS_V)
                group(g)
            step.leave(GROUPS - 1)
            group(GROUPS - 1, last=True)

        @block.gpsimd
        def _(pool):
            pool.sem_inc(s2_ok, PRIMED)
            step = Chain(pool, chain_p)
            with pool.Fori(0, GROUPS) as g:
                step.loop(g, STEPS_P)
                for i in range(2, 6):
                    pool.wait_ge(whi_ok, len(START) + 6 * g + i - 1)
                    src, hi, lo = item_parts(i)
                    pool.tensor_tensor(lo, src, hi, ALU.subtract).then_inc(itemB_ok, 1)
                pool.wait_ge(tg_in, 16 * g + 16)
                pool.wait_ge(conv_ok, PRIMED + 4 * g + 4)
                for s in range(STEPS):
                    pool.wait_ge(ring_ev, PRIMED + RING * g + RING_P + (2 if s < 2 else min(2 * s, NT)))
                    pool.wait_ge(st_mm, PRIMED + STEPS * g + max(s - 1, 0))
                    for d in range(2):
                        c = step_chunk(d, s)
                        ins = pool.tensor_tensor(per_head(xw[:, s % 2, d]), per_head(tk[:, c, 0:GC]),
                                                 bcast(tgk(T_WEND, c, d).unsqueeze(2), R, HP), ALU.mult)
                    ins.then_inc(xw_ok, 1)

                def ahead(c):
                    pool.wait_ge(seg_mm, PRIMED + LT * g + max(c - 1, 0))
                    pool.tensor_tensor(per_head(sr[:, c % 2, 0]), bcast(tgk(T_DA, c + CT, 0).unsqueeze(2), R, P),
                                       bcast(masks[:, UP].unsqueeze(1), R, P), ALU.mult).then_inc(sr_ok, 1)
                    pool.wait_ge(y_mm, PRIMED + LT * g + max(c - 1, 0))
                    for d in range(2):
                        ins = pool.tensor_tensor(per_head(dtx[:, c % 2, d]), per_head(tk[:, c + CT, 0:GC]),
                                                 bcast(tgk(T_DT, c + CT, d).unsqueeze(2), R, HP), ALU.mult)
                    ins.then_inc(dtx_ok, 1)

                pool.wait_ge(st_mm, PRIMED + STEPS * g + STEPS)
                ahead(0)
                for c in range(LT):
                    if c + 1 < LT:
                        ahead(c + 1)
                    step(pool.tensor_tensor(per_head(xd[:]), per_head(tk[:, c + CT, 0:GC]),
                                            bcast(tg[:, T_SKIP:T_ALL].unsqueeze(2), R, HP), ALU.mult))
                    pool.wait_ge(t1_ok, PRIMED + LT * g + c + 1)
                    step(pool.tensor_tensor(xd[:], xd[:], t1[:, c % 2, 0], ALU.add))
                    pool.tensor_tensor(t1[:, c % 2, 0], xd[:], t1[:, c % 2, 1], ALU.add).then_inc(s2_ok, 1)
                    pool.wait_ge(s2_ok, PRIMED + LT * g + c + 1)
            step.leave(GROUPS)


STEPS_V = 6 + 1 + 4 * (TAPS - 1) + STEPS - 1 + LT
STEPS_P = 2 * LT


def compress(k, keep, cqT, ckvT, kst):
    nc, io = k.nc, k.io
    ident, eps = keep["ident"], keep["eps"]
    with ExitStack() as st:
        sb = lambda n, s: k.sb(st, n, s)
        wc = sb("wc", [P, KD, NC_SMALL])
        hT = sb("hT_c", [P, KD, NTOK])
        cs = sb("cs", [P, NT, NC_SMALL])
        junk = sb("junk_c", [P, QL])
        ss = sb("ss_c", [P, 3, 3, NT])
        gT = sb("gT", [P, 3])
        gr = sb("gr", [P, ROPE])
        rope = sb("rope_c", [P, 2, LT, ROPE])
        kr = sb("kr", [P, NT, ROPE])
        ka = sb("ka", [P, LT, ROPE])
        kb = sb("kb", [P, LT, ROPE])
        ps = k.banks(st, "ps_c")
        sem = lambda n: k.sem(st, "c_" + n)
        w_in, par_in, mm, ev, stat, rs_ok, sc_ok, turned, out_ok, chain = (
            sem(n) for n in ("w_in", "par_in", "mm", "ev", "stat", "rs_ok", "sc_ok", "turned", "out_ok", "chain"))
        block = st.enter_context(nc.Block())
        h_in = [sem(f"h_in{t}") for t in range(NT // 2)]
        kinds = ((0, QL), (QL, QL + KVL), (QL + KVL, NC_SMALL))

        @block.sync
        def _(sp):
            sp.dma_start(wc[:], io["w_in"][0].rearrange("(k p) n -> p k n", p=P)[:, :, 0:NC_SMALL]).then_inc(w_in, 16)
            for j in range(NT // 2):
                cols = slice(2 * j * P, 2 * (j + 1) * P)
                sp.dma_start(hT[:, :, cols], io["hT"][:, :, cols].rearrange("k p n -> p k n")).then_inc(h_in[j], 16)
            for dst, src in ((gT[:, 0:2], io["q_gain"]), (gT[:, 2:3], io["kv_gain"]), (rope[:], io["rope"]),
                             (gr[:], io["qk_k_g"][0, NOPE:QKD].partition_broadcast(P))):
                sp.dma_start(dst, src).then_inc(par_in, 16)

        @block.tensor
        def _(pe):
            pe.wait_ge(w_in, 16)
            for t in range(NT):
                if t >= 4:
                    pe.wait_ge(ev, t - 3)
                lo = QL if t < CT else 0
                if t % 2 == 0:
                    pe.wait_ge(h_in[t // 2], 16)
                for kk in range(KD):
                    ins = pe.matmul(ps[:, t % 4, lo:NC_SMALL], hT[:, kk, t * P:(t + 1) * P], wc[:, kk, lo:],
                                    start=kk == 0, stop=kk == KD - 1)
                ins.then_inc(mm, 1)
            for t in range(NT):
                pe.wait_ge(sc_ok, t + 1)
                if t >= 4:
                    pe.wait_ge(out_ok, t - 3)
                for j in range(2 if t < CT else 0, 3):
                    ins = pe.transpose(ps[:, 4 + t % 4, j * P:(j + 1) * P], cs[:, t, j * P:(j + 1) * P], ident[:])
                ins.then_inc(turned, 1)

        @block.scalar
        def _(act):
            step = Chain(act, stat)
            for t in range(NT):
                lo = QL if t < CT else 0
                act.wait_ge(mm, t + 1)
                act.activation(cs[:, t, lo:], ps[:, t % 4, lo:NC_SMALL], ACT.Copy).then_inc(ev, 1)
                act.wait_ge(ev, t + 1)
                for j, (a, b) in enumerate(kinds):
                    if j > 0 or t >= CT:
                        step(act.activation(junk[:, 0:b - a], cs[:, t, a:b], ACT.Square, accum_out=ss[:, 0, j, t:t + 1]))
            for j, (a, b) in enumerate(kinds):
                lo = CT if j == 0 else 0
                step(act.activation(ss[:, 1, j, lo:], ss[:, 0, j, lo:], ACT.Ln, bias=eps[:], scale=1.0 / (b - a)))
            act.activation(ss[:, 2, 0, CT:], ss[:, 1, 0, CT:], ACT.Exp, scale=-0.5).then_inc(rs_ok, 1)
            act.activation(ss[:, 2, 1:3], ss[:, 1, 1:3], ACT.Exp, scale=-0.5).then_inc(rs_ok, 1)
            act.wait_ge(par_in, 64)
            for t in range(NT):
                act.wait_ge(turned, t + 1)
                for j in range(2 if t < CT else 0, 3):
                    dst = ckvT[:, t * P:(t + 1) * P] if j == 2 else cqT[:, j, (t - CT) * P:(t - CT + 1) * P]
                    ins = act.activation(dst, ps[:, 4 + t % 4, j * P:(j + 1) * P], ACT.Copy, scale=gT[:, j:j + 1])
                ins.then_inc(out_ok, 1)

        @block.vector
        def _(dve):
            step = Chain(dve, chain)
            dve.wait_ge(rs_ok, 2)
            for t in range(NT):
                if t >= CT:
                    dve.tensor_scalar(cs[:, t, 0:QL], cs[:, t, 0:QL], ss[:, 2, 0, t:t + 1], None, ALU.mult)
                dve.tensor_scalar(cs[:, t, QL:QL + KVL], cs[:, t, QL:QL + KVL], ss[:, 2, 1, t:t + 1], None, ALU.mult).then_inc(sc_ok, 1)
            dve.wait_ge(par_in, 64)
            step(dve.tensor_tensor(kr[:], cs[:, :, QL + KVL:], bcast(ss[:, 2, 2].unsqueeze(2), NT, ROPE), ALU.mult))
            step(dve.tensor_tensor(kr[:], kr[:], bcast(gr[:].unsqueeze(1), NT, ROPE), ALU.mult))
            step(dve.tensor_tensor(ka[:], kr[:, CT:], rope[:, 0], ALU.mult))
            halves = lambda a: a.rearrange("p t (x h y) -> p (t x) h y", x=2, h=2)
            for h in range(2):
                step(dve.tensor_tensor(halves(kb[:])[:, :, h], halves(kr[:, CT:])[:, :, 1 - h], halves(rope[:, 1])[:, :, h], ALU.mult))
            for h in range(2):
                dve.tensor_copy(kst[:, 0:CT, h, NOPE:], kr[:, 0:CT])
                step(dve.tensor_tensor(kst[:, CT:, h, NOPE:], ka[:], kb[:], ALU.add))


KEY_SEGS = ((0, 512), (512, 512), (1024, 256))


class Bank:

    def __init__(self, full, empty, at):
        self.full, self.empty, self.at = full, empty, at

    def fill(self, pe):
        pe.wait_ge(self.empty.sem, self.empty.value())
        return self.at

    def filled(self, ins):
        self.full.raised(ins)
        self.empty.add()

    def take(self, eng):
        eng.wait_ge(self.full.sem, self.full.add())
        return self.at

    def emptied(self, ins):
        self.empty.raised(ins)

    def skip(self, n=1):
        self.full.add(n)
        self.empty.add(n)


QB = 512
BLOCKS = 2 * NLAT // QB
QT4 = QB // P
PRING = 5


def attention(k, keep, cqT, ckvT, kst):
    nc, io = k.nc, k.io
    ident, eps = keep["ident"], keep["eps"]
    QW, KW = 2 * QKD, 2 * (NOPE + VD)
    with ExitStack() as st:
        sb = lambda n, s, dt=F32: k.sb(st, n, s, dt)
        sem = lambda n: k.sem(st, "a_" + n)
        wq = sb("wq", [P, 2, 2, QW])
        wkv = sb("wkv", [P, 2, KW])
        q = sb("q", [P, LT, QW])
        kn = sb("kn", [P, NT, 2, NOPE])
        vst = sb("vst", [P, 2, NT, 3, VD])
        sq = sb("sq", [P, LT * QW])
        rope = sb("rope_a", [P, 2, LT, ROPE])
        qa = sb("qa", [P, LT, 2, ROPE])
        qb = sb("qb", [P, LT, 2, ROPE])
        gr = sb("gr_a", [P, ROPE])
        gT = sb("gT_a", [P, 2])
        ss = sb("ss_a", [P, 3, 4 * LT + 2 * NT])
        one = sb("one_a", [P, VD])
        QH = sb("QH", [P, 2, 2, NLAT], F32R)
        QLo = sb("QLo", [P, 2, 2, NLAT], F32R)
        KH = sb("KH", [P, 2, 2, NTOK], F32R)
        KL = sb("KL", [P, 2, 2, NTOK], F32R)
        pT = sb("pT", [P, PRING, QB])
        raw_o = sb("raw_o", [P, QB])
        sums_o = sb("sums_o", [P, QB])
        inv_o = sb("inv_o", [P, QB])
        att = sb("att", [P, 2, NLAT])
        mx = sb("mx", [P, QT4])
        ps = k.banks(st, "ps_a")
        w_in = [sem(f"w_in{b}") for b in range(2)]
        att_out = [sem(f"att_out{b}") for b in range(2)]
        par_in, one_ok = sem("par_in"), sem("one_ok")
        full = [sem("full6"), sem("full7")]
        empty = [sem("empty6"), sem("empty7")]
        sqq, redq, sqk, redk, rs_ok, qk_ok, hi_ok = (sem(n) for n in ("sqq", "redq", "sqk", "redk", "rs_ok", "qk_ok", "hi_ok"))
        max_mm, max_ok, s_mm, exp_ok, pv_ok, norm_ok = (sem(n) for n in ("max_mm", "max_ok", "s_mm", "exp_ok", "pv_ok", "norm_ok"))
        raw_ok, sums_ok, inv_ok = sem("raw_ok"), sem("sums_ok"), sem("inv_ok")
        chain_v, chain_a = sem("chain_v"), sem("chain_a")
        block = st.enter_context(nc.Block())
        NQ, NK = 2 * LT, 2 * NT
        cut_q, cut_k, cut_r = slice(0, NQ), slice(NQ, NQ + NK), slice(NQ + NK, 2 * NQ + NK)

        def banks():
            return [Bank(Count(full[j]), Count(empty[j]), ps[:, 6 + j]) for j in range(2)]

        def part(h):
            return slice(VD * h, VD * h + VD)

        proj = [("q", t) for t in range(0, LT, 2)] + [("kv", t) for t in range(0, NT, 2)]
        turns = [("q", h, t, 4) for h in range(2) for t in range(0, LT, 4)] + \
                [("k", h, t, min(4, NT - t)) for h in range(2) for t in range(0, NT, 4)]
        JOBS = (2 * ((len(proj) + 1) // 2 + len(turns) // 2 + BLOCKS), 2 * (len(proj) // 2 + len(turns) // 2))

        class Walk:

            def __init__(self, loops):
                self.loops = loops

            def pair(self, p, b, more):
                for n in range(BLOCKS):
                    nxt = (b, n + 1) if n < BLOCKS - 1 else (1 - b, 0) if more else None
                    for m in range(NT + 2):
                        self.chunk(b, n, m)
                        if nxt and m in (1, 4, 6, 8):
                            self.maxima(*nxt, m // 2 - (m > 1))
                        if more and n == 0 and 1 <= m <= len(proj):
                            self.project(1 - b, m - 1)
                        if more and (n, m) == (0, NT):
                            self.square()
                        if more and n == 1:
                            if m == 1:
                                self.reduce_q()
                            if m == 3:
                                self.reduce_k()
                            if m == 4:
                                self.rstd()
                            if m in (5, 7, 8):
                                self.scale((5, 7, 8).index(m))
                        if more and n == 2 and 1 <= m <= len(turns):
                            self.turn(1 - b, m - 1)
                        if nxt and m == NT:
                            self.row(*nxt)
                    self.norm(p, b, n)

            def all(self, eng):
                for j in range(len(proj)):
                    self.project(0, j)
                self.square()
                self.reduce_q()
                self.reduce_k()
                self.rstd()
                for part in range(3):
                    self.scale(part)
                for j in range(len(turns)):
                    self.turn(0, j)
                for t in range(QT4):
                    self.maxima(0, 0, t)
                self.row(0, 0)
                loop_turns = PAIRS // 2 - 1
                with eng.Fori(0, loop_turns) as i:
                    for c, per in self.loops:
                        c.loop(i, per)
                    self.pair(2 * i, 0, True)
                    self.pair(2 * i + 1, 1, True)
                for c, _ in self.loops:
                    c.leave(loop_turns)
                self.pair(PAIRS - 2, 0, True)
                self.pair(PAIRS - 1, 1, False)

            def skip(self, *_):
                pass
            chunk = maxima = square = reduce_q = reduce_k = rstd = scale = norm = skip

            def project(self, b, j):
                self.bk[j % 2].skip()

            def turn(self, b, j):
                self.bk[j % 2].skip()

            def row(self, b, n):
                self.bk[0].skip()

        @block.sync
        def _(sp):
            def loads(p, b):
                sp.dma_start(wq[:, b], io["w_uq"][0].rearrange("(k p) n -> p k n", p=P)[:, :, bass.ds(p * QW, QW)]).then_inc(w_in[b], 16)
                sp.wait_ge(w_in[b], 32 * (p // 2) + 16 if isinstance(p, int) else 16 * (p - b) + 16)
                sp.dma_start(wkv[:, b], io["w_ukv"][0, :, bass.ds(p * KW, KW)]).then_inc(w_in[b], 16)

            def store(p, b, blocks_done):
                sp.wait_ge(norm_ok, PRIMED + blocks_done)
                sp.dma_start(io["attT"][bass.ds(p, 1)].rearrange("a p n -> p (a n)"), att[:, b]).then_inc(att_out[b], 16)
            for b in range(2):
                sp.sem_inc(att_out[b], PRIMED)
            sp.dma_start(rope[:], io["rope"]).then_inc(par_in, 16)
            sp.dma_start(gr[:], io["qk_q_g"][0, NOPE:QKD].partition_broadcast(P)).then_inc(par_in, 16)
            sp.wait_ge(one_ok, 1)
            sp.dma_start(gT[0:NOPE, :], io["qk_gain"][0:NOPE]).then_inc(par_in, 16)
            loads(0, 0)
            loads(1, 1)
            with sp.Fori(1, PAIRS // 2) as i:
                for b in range(2):
                    sp.wait_ge(qk_ok, 2 * i + b - 1)
                    loads(2 * i + b, b)
                    store(2 * i + b - 2, b, BLOCKS * (2 * i + b - 1))
            for b in range(2):
                store(PAIRS - 2 + b, b, BLOCKS * (PAIRS - 1 + b))
                sp.wait_ge(att_out[b], PRIMED + 16 * (PAIRS // 2))

        @block.tensor
        def _(pe):
            bk = banks()
            mm_, mo, sm, ex = Count(max_mm), Count(max_ok, primed=PRIMED), Count(s_mm), Count(exp_ok)
            pv, qk = Count(pv_ok, primed=PRIMED), Count(qk_ok)
            ra, su = Count(raw_ok, primed=PRIMED), Count(sums_ok, primed=PRIMED)
            wi = [Count(w_in[b], 32) for b in range(2)]
            pe.wait_ge(one_ok, 2)

            class Pe(Walk):
                def project(self, b, j):
                    kind, t = proj[j]
                    if j == 0:
                        pe.wait_ge(w_in[b], wi[b].add())
                    o = bk[j % 2].fill(pe)
                    for h in range(2):
                        if kind == "q":
                            for kk in range(2):
                                ins = pe.matmul(o[:, h * QW:(h + 1) * QW], cqT[:, kk, (t + h) * P:(t + h + 1) * P],
                                                wq[:, b, kk], start=kk == 0, stop=kk == 1)
                        else:
                            ins = pe.matmul(o[:, h * KW:(h + 1) * KW], ckvT[:, (t + h) * P:(t + h + 1) * P],
                                            wkv[:, b], start=True, stop=True)
                    bk[j % 2].filled(ins)

                def turn(self, b, j):
                    kind, h, t, cnt = turns[j]
                    if j == 0:
                        pe.wait_ge(qk_ok, qk.add())
                    o = bk[j % 2].fill(pe)
                    for i in range(cnt):
                        src = q[:, t + i, h * QKD:(h + 1) * QKD] if kind == "q" else kst[:, t + i, h]
                        ins = pe.transpose(o[0:QKD, i * P:(i + 1) * P], src, ident[:])
                    bk[j % 2].filled(ins)

                def maxima(self, b, n, t):
                    h, q0 = n // 2, (n % 2) * QB + t * P
                    if t == 0 and n == 0:
                        for j in range(2):
                            pe.wait_ge(empty[j], bk[j].empty.value())
                    pe.wait_ge(max_ok, mo.value())
                    for j, (c0, wd) in enumerate(KEY_SEGS):
                        ins = pe.matmul(ps[:, j, 0:wd], QH[0:QKD, b, h, q0:q0 + P], KH[0:QKD, b, h, c0:c0 + wd], start=True, stop=True)
                    mm_.raised(ins)
                    mo.add()

                def row(self, b, n):
                    o = bk[0].fill(pe)
                    pe.wait_ge(max_ok, mo.value())
                    for t in range(QT4):
                        ins = pe.matmul(o[0:1, t * P:(t + 1) * P], mx[:, t:t + 1], ident[:], start=True, stop=True)
                    bk[0].filled(ins)

                def chunk(self, b, n, m):
                    h, q0 = n // 2, (n % 2) * QB
                    cols = slice(q0, q0 + QB)
                    if m == 0:
                        pe.wait_ge(empty[0], bk[0].empty.value())
                    if m < NT:
                        if m >= 2:
                            pe.wait_ge(exp_ok, ex.value(-(m - 1)))
                        o, keys = ps[:, 3 + m % 2], slice(m * P, (m + 1) * P)
                        pe.matmul(o, KH[0:QKD + 1, b, h, keys], QH[0:QKD + 1, b, h, cols], start=True, stop=False)
                        pe.matmul(o, KL[0:QKD, b, h, keys], QH[0:QKD, b, h, cols], start=False, stop=False)
                        sm.raised(pe.matmul(o, KH[0:QKD, b, h, keys], QLo[0:QKD, b, h, cols], start=False, stop=True))
                    if m >= 2:
                        c = m - 2
                        if c == 0:
                            pe.wait_ge(raw_ok, ra.value())
                            pe.wait_ge(sums_ok, su.value())
                        pe.wait_ge(exp_ok, ex.value(-(c + 1)))
                        pv.raised(pe.matmul(ps[:, 5], vst[:, b, c, h:h + 2].rearrange("p a n -> p (a n)"), pT[:, c % PRING],
                                            start=c == 0, stop=c == NT - 1))

                def norm(self, p, b, n):
                    ex.add(NT)
                    ra.add()
                    su.add()

            walk = Pe([(bk[0].full, JOBS[0]), (bk[0].empty, JOBS[0]), (bk[1].full, JOBS[1]), (bk[1].empty, JOBS[1]),
                       (mm_, 2 * QT4 * BLOCKS), (mo, 2 * QT4 * BLOCKS), (sm, 2 * NT * BLOCKS), (ex, 2 * NT * BLOCKS),
                       (pv, 2 * NT * BLOCKS), (ra, 2 * BLOCKS), (su, 2 * BLOCKS), (qk, 2), (wi[0], 1), (wi[1], 1)])
            walk.bk = bk
            walk.all(pe)

        @block.scalar
        def _(act):
            bk = banks()
            rk, rs, hi = Count(redk), Count(rs_ok), Count(hi_ok)
            sm, ex, pv = Count(s_mm), Count(exp_ok), Count(pv_ok, primed=PRIMED)
            iv, su = Count(inv_ok, primed=PRIMED), Count(sums_ok, primed=PRIMED)
            act.sem_inc(pv_ok, PRIMED)
            act.sem_inc(sums_ok, PRIMED)
            step = Chain(act, chain_a)
            act.wait_ge(par_in, 48)

            class Act(Walk):
                def project(self, b, j):
                    if j % 2:
                        bk[1].skip()
                        return
                    o, (kind, t) = bk[0].take(act), proj[j]
                    if kind == "q":
                        ins = act.activation(q[:, t:t + 2], o[:, 0:2 * QW].rearrange("p (t n) -> p t n", t=2), ACT.Copy)
                    else:
                        o = o.rearrange("p (t h two x) -> p t h two x", t=2, h=2, two=2)
                        for h in range(2):
                            act.activation(kn[:, t:t + 2, h], o[:, :, h, 0], ACT.Copy)
                            ins = act.activation(vst[:, b, t:t + 2, 2 * h], o[:, :, h, 1], ACT.Copy)
                    bk[0].emptied(ins)

                def rstd(self):
                    act.wait_ge(redk, rk.add())
                    step(act.activation(ss[:, 1, 0:NQ + NK], ss[:, 0, 0:NQ + NK], ACT.Ln, bias=eps[:], scale=1.0 / NOPE))
                    step(act.activation(ss[:, 1, cut_r], ss[:, 0, cut_r], ACT.Ln, bias=eps[:], scale=1.0 / ROPE))
                    rs.raised(act.activation(ss[:, 2], ss[:, 1], ACT.Exp, scale=-0.5))

                def turn(self, b, j):
                    kind, h, t, cnt = turns[j]
                    o = bk[j % 2].take(act)
                    bk[j % 2].empty.add()
                    dst, g = (QH, 0) if kind == "q" else (KH, 1)
                    hi.raised(act.activation(dst[0:QKD, b, h, t * P:(t + cnt) * P], o[0:QKD, 0:cnt * P], ACT.Copy,
                                             scale=gT[0:QKD, g:g + 1]))

                def chunk(self, b, n, m):
                    if m < NT:
                        act.wait_ge(s_mm, sm.add())
                        act.wait_ge(pv_ok, pv.value() if m < PRING else pv.value(-(m - PRING + 1)))
                        ex.raised(act.activation(pT[:, m % PRING], ps[:, 3 + m % 2], ACT.Exp, scale=SCALE))

                def norm(self, p, b, n):
                    act.wait_ge(pv_ok, pv.add(NT))
                    act.wait_ge(inv_ok, iv.value())
                    iv.add()
                    su.raised(act.activation(sums_o[part(n // 2)], ps[part(1 - n // 2), 5], ACT.Copy))

            walk = Act([(bk[0].full, JOBS[0]), (bk[0].empty, JOBS[0]), (bk[1].full, JOBS[1]), (bk[1].empty, JOBS[1]),
                        (sm, 2 * NT * BLOCKS), (ex, 2 * NT * BLOCKS), (pv, 2 * NT * BLOCKS), (rk, 2), (rs, 2),
                        (iv, 2 * BLOCKS), (su, 2 * BLOCKS),
                        (hi, 2 * len(turns)), (step, 4)])
            walk.bk = bk
            walk.all(act)

        @block.vector
        def _(dve):
            bk = banks()
            mm_, mo, pv = Count(max_mm), Count(max_ok, primed=PRIMED), Count(pv_ok, primed=PRIMED)
            no, ra = Count(norm_ok, primed=PRIMED), Count(raw_ok, primed=PRIMED)
            iv, su = Count(inv_ok, primed=PRIMED), Count(sums_ok, primed=PRIMED)
            sq1, sq2, r1, r2, qk, rs, hi = Count(sqq), Count(sqk), Count(redq), Count(redk), Count(qk_ok), Count(rs_ok), Count(hi_ok)
            step = Chain(dve, chain_v)
            dve.sem_inc(max_ok, PRIMED)
            dve.sem_inc(raw_ok, PRIMED)
            dve.sem_inc(inv_ok, PRIMED)
            step(dve.memset(one[:], 1.0))
            dve.memset(gT[:], 1.0).then_inc(one_ok, 1)
            for b in range(2):
                dve.memset(vst[:, b, :, 1], 1.0)
                for h in range(2):
                    ins = dve.tensor_copy(KH[QKD:QKD + 1, b, h].rearrange("p (a n) -> p a n", n=VD),
                                          bcast(one[QKD:QKD + 1].unsqueeze(1), NTOK // VD, VD))
            ins.then_inc(one_ok, 1)
            dve.wait_ge(par_in, 48)

            class Dve(Walk):
                def project(self, b, j):
                    if j % 2 == 0:
                        bk[0].skip()
                        return
                    o, (kind, t) = bk[1].take(dve), proj[j]
                    if kind == "q":
                        ins = dve.tensor_copy(q[:, t:t + 2], o[:, 0:2 * QW].rearrange("p (t n) -> p t n", t=2))
                    else:
                        o = o.rearrange("p (t h two x) -> p t h two x", t=2, h=2, two=2)
                        for h in range(2):
                            dve.tensor_copy(kn[:, t:t + 2, h], o[:, :, h, 0])
                            ins = dve.tensor_copy(vst[:, b, t:t + 2, 2 * h], o[:, :, h, 1])
                    bk[1].emptied(ins)

                def reduce_q(self):
                    dve.wait_ge(sqq, sq1.add())
                    rows = sq[:].rearrange("p (n x) -> p n x", x=QKD)
                    dve.tensor_reduce(ss[:, 0, cut_q], rows[:, :, 0:NOPE], AX_X, ALU.add)
                    r1.raised(dve.tensor_reduce(ss[:, 0, cut_r], rows[:, :, NOPE:], AX_X, ALU.add))

                def reduce_k(self):
                    dve.wait_ge(sqk, sq2.add())
                    r2.raised(dve.tensor_reduce(ss[:, 0, cut_k], sq[:, 0:NK * NOPE].rearrange("p (n x) -> p n x", x=NOPE), AX_X, ALU.add))

                def scale(self, part):
                    rows = q[:].rearrange("p t (h x) -> p (t h) x", h=2)
                    turn = rows[:, :, NOPE:]
                    q4 = q[:].rearrange("p t (h x) -> p t h x", h=2)[:, :, :, NOPE:]
                    if part == 0:
                        dve.wait_ge(rs_ok, rs.add())
                        dve.tensor_tensor(rows[:, :, 0:NOPE], rows[:, :, 0:NOPE], bcast(ss[:, 2, cut_q].unsqueeze(2), NQ, NOPE), ALU.mult)
                        step(dve.tensor_tensor(turn, turn, bcast(ss[:, 2, cut_r].unsqueeze(2), NQ, ROPE), ALU.mult))
                        step(dve.tensor_tensor(turn, turn, bcast(gr[:].unsqueeze(1), NQ, ROPE), ALU.mult))
                    elif part == 1:
                        dve.tensor_tensor(qa[:], q4, bcast(rope[:, 0].unsqueeze(2), LT, 2, ROPE), ALU.mult)
                        halves = lambda a: a.rearrange("p t (x h y) -> p t x h y", x=2, h=2)
                        for h in range(2):
                            for e in range(2):
                                ins = dve.tensor_tensor(halves(qb[:, :, h])[:, :, :, e], halves(q4[:, :, h])[:, :, :, 1 - e],
                                                        halves(rope[:, 1])[:, :, :, e], ALU.mult)
                        step(ins)
                    else:
                        dve.tensor_tensor(turn, qa[:].rearrange("p t h x -> p (t h) x"), qb[:].rearrange("p t h x -> p (t h) x"), ALU.add)
                        qk.raised(dve.tensor_tensor(kst[:].rearrange("p t h x -> p (t h) x")[:, :, 0:NOPE], kn[:].rearrange("p t h x -> p (t h) x"),
                                                    bcast(ss[:, 2, cut_k].unsqueeze(2), NK, NOPE), ALU.mult))

                def turn(self, b, j):
                    kind, h, t, cnt = turns[j]
                    o = bk[j % 2].take(dve)
                    dve.wait_ge(hi_ok, hi.add())
                    (top, rest), g = ((QH, QLo), 0) if kind == "q" else ((KH, KL), 1)
                    cols = slice(t * P, (t + cnt) * P)
                    bk[j % 2].emptied(dve.scalar_tensor_tensor(rest[0:QKD, b, h, cols], o[0:QKD, 0:cnt * P], gT[0:QKD, g:g + 1],
                                                               top[0:QKD, b, h, cols], ALU.mult, ALU.subtract))

                def maxima(self, b, n, t):
                    dve.wait_ge(max_mm, mm_.add())
                    mo.raised(dve.tensor_reduce(mx[:, t:t + 1], ps[:, 0:3].rearrange("p b n -> p (b n)")[:, 0:NTOK], AX_X, ALU.max))

                def row(self, b, n):
                    o = bk[0].take(dve)
                    bk[0].emptied(dve.tensor_scalar(QH[QKD:QKD + 1, b, n // 2, (n % 2) * QB:(n % 2) * QB + QB], o[0:1], -1.0, None, ALU.mult))

                def norm(self, p, b, n):
                    dve.wait_ge(pv_ok, pv.add(NT))
                    dve.wait_ge(norm_ok, no.value())
                    no.add()
                    ra.raised(dve.tensor_copy(raw_o[part(n // 2)], ps[part(n // 2), 5]))
                    dve.wait_ge(sums_ok, su.add())
                    iv.raised(dve.reciprocal(inv_o[part(n // 2)], sums_o[part(n // 2)]))

            walk = Dve([(bk[0].full, JOBS[0]), (bk[0].empty, JOBS[0]), (bk[1].full, JOBS[1]), (bk[1].empty, JOBS[1]),
                        (mm_, 2 * QT4 * BLOCKS), (mo, 2 * QT4 * BLOCKS), (pv, 2 * NT * BLOCKS), (no, 2 * BLOCKS), (rs, 2),
                        (sq1, 2), (sq2, 2), (r1, 2), (r2, 2), (qk, 2), (hi, 2 * len(turns)), (ra, 2 * BLOCKS), (iv, 2 * BLOCKS), (su, 2 * BLOCKS),
                        (step, 2 * 3)])
            walk.bk = bk
            walk.all(dve)

        @block.gpsimd
        def _(pool):
            bk = banks()
            s1, s2, r1 = Count(sqq), Count(sqk), Count(redq)
            no, ra, iv = Count(norm_ok, primed=PRIMED), Count(raw_ok, primed=PRIMED), Count(inv_ok, primed=PRIMED)
            ao = [Count(att_out[b], 16, primed=PRIMED) for b in range(2)]
            pool.sem_inc(norm_ok, PRIMED)

            class Pool(Walk):
                def square(self):
                    for j in range(2):
                        pool.wait_ge(empty[j], bk[j].empty.value())
                    s1.raised(pool.tensor_tensor(sq[:], q[:].rearrange("p t x -> p (t x)"), q[:].rearrange("p t x -> p (t x)"), ALU.mult))
                    pool.wait_ge(redq, r1.add())
                    rows = kn[:].rearrange("p t h x -> p (t h x)")
                    s2.raised(pool.tensor_tensor(sq[:, 0:NK * NOPE], rows, rows, ALU.mult))

                def norm(self, p, b, n):
                    pool.wait_ge(raw_ok, ra.add())
                    pool.wait_ge(inv_ok, iv.add())
                    if n == 0:
                        pool.wait_ge(att_out[b], ao[b].value())
                        ao[b].add()
                    mine = part(n // 2)
                    no.raised(pool.tensor_tensor(att[mine, b, (n % 2) * QB:(n % 2) * QB + QB], raw_o[mine], inv_o[mine], ALU.mult))
                    pool.wait_ge(norm_ok, no.value())

            walk = Pool([(bk[0].full, JOBS[0]), (bk[0].empty, JOBS[0]), (bk[1].full, JOBS[1]), (bk[1].empty, JOBS[1]), (s1, 2), (s2, 2), (r1, 2),
                         (no, 2 * BLOCKS), (ra, 2 * BLOCKS), (iv, 2 * BLOCKS), (ao[0], 1), (ao[1], 1)])
            walk.bk = bk
            walk.all(pool)


def merge(k, keep):
    nc, io = k.nc, k.io
    w = io["w_in"][0].rearrange("(k p) n -> p k n", p=P)
    wab = io["w_late"].rearrange("(k p) n -> p k n", p=P)
    wa, wb = wab[:, KD:2 * KD], wab[:, 2 * KD:]
    with ExitStack() as st:
        sem = lambda n: k.sem(st, "g_" + n)
        hT = k.sb(st, "hT_m", [P, KD, NLAT])
        attT = k.sb(st, "attT", [P, PAIRS, NLAT])
        uT = k.sb(st, "uT", [P, 2 * GROUPS, NLAT])
        ws = k.sb(st, "ws", [P, 5, KD, P])
        sig = k.sb(st, "sig", [P, 2, 2, 512])
        wm = k.sb(st, "wm_late", [P, KD, 512])
        part = k.sb(st, "part_g", [P, 512])
        brow = k.sb(st, "brow", [P, 512])
        row = k.sb(st, "row_g", [P, 512])
        ones = k.sb(st, "ones_g", [P, P])
        mo = k.sb(st, "mo", [P, NLAT])
        ps = k.banks(st, "ps_m")
        w_in = [sem(f"w_in{j}") for j in range(5)]
        u_in = [sem(f"u_in{j}") for j in range(4)]
        a_in = [sem(f"a_in{j}") for j in range(2)]
        h_in = [sem(f"h_in{j}") for j in range(KD)]
        mm, sig_ok, prod, merged, mo_out = sem("mm"), sem("sig_ok"), sem("prod"), sem("merged"), sem("mo_out")
        wm_in, b_in, part_ok, row_mm, row_ok, row_out, chain, ones_ok = (
            sem(n) for n in ("wm_in", "b_in", "part_ok", "row_mm", "row_ok", "row_out", "chain", "ones_ok"))
        block = st.enter_context(nc.Block())

        @block.sync
        def _(sp):
            def loads(m, first):
                for j, (src, col, done) in enumerate(((w, COL_GA, 2), (w, COL_GB, 4), (wa, 0, 6), (wb[:, 0:KD], 0, 8), (wb[:, KD:], 0, 8))):
                    if not first:
                        sp.wait_ge(mm, 8 * m - 8 + done)
                    sp.dma_start(ws[:, j], src[:, :, bass.ds(col + m * P, P)]).then_inc(w_in[j], 16)
            wl = io["w_mod_late"].rearrange("(k p) n -> p k n", p=P)

            def late(m, first):
                if not first:
                    sp.wait_ge(row_ok, PRIMED + m)
                sp.dma_start(wm[:], wl[:, :, bass.ds(m * 512, 512)]).then_inc(wm_in, 16)
                sp.dma_start(brow[:], io["b_mod_late"][bass.ds(m * 512, 512)].partition_broadcast(P)).then_inc(b_in, 16)
            for j in range(KD):
                sp.dma_start(hT[:, j], io["hT"][j, :, NCTX:]).then_inc(h_in[j], 16)
                if j == 0:
                    loads(0, True)
            late(0, True)
            for j in range(2):
                sp.dma_start(attT[:, 4 * j:4 * j + 4], io["attT"][4 * j:4 * j + 4].rearrange("t p n -> p t n")).then_inc(a_in[j], 16)
            for j in range(4):
                sp.dma_start(uT[:, 4 * j:4 * j + 4], io["uT"][4 * j:4 * j + 4].rearrange("t p n -> p t n")).then_inc(u_in[j], 16)
            sp.sem_inc(mo_out, PRIMED)
            sp.sem_inc(row_out, PRIMED)

            def store(m):
                sp.wait_ge(row_ok, PRIMED + m + 1)
                sp.dma_start(io["mod_rows"][bass.ds(m, 1)].rearrange("a p n -> p (a n)"), row[:]).then_inc(row_out, 16)
                sp.wait_ge(merged, PRIMED + 2 * m + 2)
                sp.dma_start(io["mT"][bass.ds(m, 1)].rearrange("a p n -> p (a n)"), mo[:]).then_inc(mo_out, 16)
            with sp.Fori(0, KD - 1) as m:
                loads(m + 1, False)
                late(m + 1, False)
                store(m)
            store(KD - 1)
            sp.wait_ge(mo_out, PRIMED + 16 * KD)
            sp.wait_ge(row_out, PRIMED + 16 * KD)

        @block.tensor
        def _(pe):
            pe.wait_ge(ones_ok, 1)
            with pe.Fori(0, KD) as m:
                for kind in range(4):
                    pe.wait_ge(w_in[kind], 16 * m + 16)
                    if kind == 2:
                        for j in range(2):
                            pe.wait_ge(a_in[j], 16)
                    if kind == 3:
                        pe.wait_ge(part_ok, m + 1)
                        pe.wait_ge(sig_ok, PRIMED + 4 * m + 1)
                        pe.matmul(ps[:, 0], ones[:], part[:], start=True, stop=True).then_inc(row_mm, 1)
                        pe.wait_ge(w_in[4], 16 * m + 16)
                        for j in range(4):
                            pe.wait_ge(u_in[j], 16)
                    for half in range(2):
                        if kind < 2:
                            pe.wait_ge(sig_ok, PRIMED + 4 * m)
                            if kind == 0 and half == 0:
                                pe.wait_ge(row_ok, PRIMED + m)
                        else:
                            pe.wait_ge(prod, PRIMED + 4 * m)
                        o = ps[:, 2 * kind + half]
                        cols = slice(half * 512, half * 512 + 512)
                        for kk in range(2 * KD if kind == 3 else KD):
                            if kind == 0 and half == 0:
                                pe.wait_ge(h_in[kk], 16)
                            lhs = ws[:, kind + kk // KD, kk % KD]
                            rhs = (hT[:, kk, cols] if kind < 2 else
                                   attT[:, kk, cols] if kind == 2 else uT[:, kk, cols])
                            ins = pe.matmul(o, lhs, rhs, start=kk == 0, stop=kk == (2 * KD if kind == 3 else KD) - 1)
                        ins.then_inc(mm, 1)

        @block.scalar
        def _(act):
            act.sem_inc(sig_ok, PRIMED)
            with act.Fori(0, KD) as m:
                act.wait_ge(merged, PRIMED + 2 * m)
                for kind in range(2):
                    for half in range(2):
                        act.wait_ge(mm, 8 * m + 2 * kind + half + 1)
                        act.activation(sig[:, kind, half], ps[:, 2 * kind + half], ACT.Sigmoid).then_inc(sig_ok, 1)

        @block.vector
        def _(dve):
            dve.sem_inc(prod, PRIMED)
            dve.sem_inc(row_ok, PRIMED)
            dve.memset(ones[:], 1.0).then_inc(ones_ok, 1)
            step = Chain(dve, chain)
            act_c = keep["act_c"]
            with dve.Fori(0, KD) as m:
                step.loop(m, KD - 1)
                dve.wait_ge(wm_in, 16 * m + 16)
                step(dve.tensor_scalar(part[:], wm[:, 0], act_c[:, 0, 0:1], None, ALU.mult))
                for kk in range(1, KD):
                    ins = dve.scalar_tensor_tensor(part[:], wm[:, kk], act_c[:, kk, 0:1], part[:], ALU.mult, ALU.add)
                    if kk < KD - 1:
                        step(ins)
                ins.then_inc(part_ok, 1)
                for kind in range(2):
                    for half in range(2):
                        dve.wait_ge(mm, 8 * m + 4 + 2 * kind + half + 1)
                        dve.wait_ge(sig_ok, PRIMED + 4 * m + 2 * kind + half + 1)
                        dve.tensor_tensor(sig[:, kind, half], ps[:, 4 + 2 * kind + half], sig[:, kind, half], ALU.mult).then_inc(prod, 1)
                    if kind == 0:
                        dve.wait_ge(row_mm, m + 1)
                        dve.wait_ge(b_in, 16 * m + 16)
                        dve.wait_ge(row_out, PRIMED + 16 * m)
                        dve.tensor_tensor(row[:], ps[:, 0], brow[:], ALU.add).then_inc(row_ok, 1)
            step.leave(KD)

        @block.gpsimd
        def _(pool):
            pool.sem_inc(merged, PRIMED)
            with pool.Fori(0, KD) as m:
                pool.wait_ge(mo_out, PRIMED + 16 * m)
                for half in range(2):
                    pool.wait_ge(prod, PRIMED + 4 * m + 3 + half)
                    pool.tensor_tensor(mo[:, half * 512:half * 512 + 512],
                                       sig[:, 0, half], sig[:, 1, half], ALU.add).then_inc(merged, 1)


def out_norm(k, keep, x1, hH, hL, gate2):
    nc, io = k.nc, k.io
    modT, ident, eps = keep["modT"], keep["ident"], keep["eps"]
    with ExitStack() as st:
        sem = lambda n: k.sem(st, "o_" + n)
        wo = k.sb(st, "wo", [P, KD, D])
        mT = k.sb(st, "mT", [P, 4, KD, P])
        gate1 = k.sb(st, "gate1", [P, D])
        xt = k.sb(st, "xt_o", [P, 2, D])
        xn = k.sb(st, "xn_o", [P, 2, D])
        h2 = k.sb(st, "h2_o", [P, 2, 512])
        ss = k.sb(st, "ss_o", [P, 3, LT])
        n2 = k.sb(st, "n2", [P, KD])
        mrow = k.sb(st, "mrow", [2 * KD, P])
        ps = k.banks(st, "ps_o")
        x_in = [sem(f"x_in{j}") for j in range(2)]
        m_in = [sem(f"m_in{j}") for j in range(4)]
        w_in = [sem(f"w_in{j}") for j in range(2)]
        g_in = [sem(f"g_in{j}") for j in range(2)]
        mod_in = [sem(f"mod_in{j}") for j in range(5)]
        mod_mm, mod_ok = sem("mod_mm"), sem("mod_ok")
        mm, x1_ok, rs_ok, xn_ok, turned, ev_a, ev_v, chain_v, chain_a = (
            sem(n) for n in ("mm", "x1_ok", "rs_ok", "xn_ok", "turned", "ev_a", "ev_v", "chain_v", "chain_a"))
        hi_ok, lo_ok = sem("hi_ok"), sem("lo_ok")
        block = st.enter_context(nc.Block())

        @block.sync
        def _(sp):
            w = io["w_late"][0:D].rearrange("(k p) n -> p k n", p=P)
            mt = io["mT"].rearrange("k p n -> p k n")

            def tile(t):
                if t >= 4:
                    sp.wait_ge(mm, 2 * t - 6)
                sp.dma_start(mT[:, t % 4], mt[:, :, t * P:(t + 1) * P]).then_inc(m_in[t % 4], 16)
            tile(0)
            for b in range(4):
                sp.dma_start(mrow[4 * b:4 * b + 4], io["mod_rows"][b, 0].rearrange("(k p) -> k p", p=P)).then_inc(mod_in[b], 16)
            sp.dma_start(n2[:], io["norm2"]).then_inc(mod_in[4], 16)
            for half in range(2):
                sp.dma_start(wo[:, :, half * 512:half * 512 + 512], w[:, :, half * 512:half * 512 + 512]).then_inc(w_in[half], 16)
            rows = io["mod_rows"]
            for j, dst in enumerate((gate1, gate2)):
                sp.dma_start(dst[:].rearrange("p (b n) -> p b n", b=2), rows[4 + 2 * j:6 + 2 * j].rearrange("b p n -> p b n")).then_inc(g_in[j], 16)
            for t in range(LT):
                if t + 1 < LT:
                    tile(t + 1)
                if t >= 2:
                    sp.wait_ge(x1_ok, t - 1)
                sp.dma_start(xt[:, t % 2], io["x"][0, t * P:(t + 1) * P]).then_inc(x_in[t % 2], 16)
            sp.wait_ge(g_in[1], 16)

        @block.tensor
        def _(pe):
            def turn(t):
                pe.wait_ge(xn_ok, t + 1)
                if t == 0:
                    pe.wait_ge(mod_ok, 1)
                if t >= 2:
                    pe.wait_ge(ev_a, t - 1)
                    pe.wait_ge(ev_v, t - 1)
                for h in range(2):
                    for j in range(4):
                        ins = pe.transpose(ps[:, 4 + 2 * (t % 2) + h, j * P:(j + 1) * P],
                                           xn[:, t % 2, (4 * h + j) * P:(4 * h + j + 1) * P], ident[:])
                    ins.then_inc(turned, 1)
            for b in range(4):
                pe.wait_ge(mod_in[b], 16)
            pe.transpose(ps[:, 4, 0:2 * KD], mrow[:], ident[0:2 * KD, 0:2 * KD]).then_inc(mod_mm, 1)
            for t in range(LT):
                if t >= 2:
                    pe.wait_ge(x1_ok, t - 1)
                pe.wait_ge(m_in[t % 4], 16 * (t // 4 + 1))
                for half in range(2):
                    pe.wait_ge(w_in[half], 16)
                    for kk in range(KD):
                        ins = pe.matmul(ps[:, 2 * (t % 2) + half], mT[:, t % 4, kk], wo[:, kk, half * 512:half * 512 + 512],
                                        start=kk == 0, stop=kk == KD - 1)
                    ins.then_inc(mm, 1)
                if t >= 1:
                    turn(t - 1)
            turn(LT - 1)

        @block.vector
        def _(dve):
            step = Chain(dve, chain_v)

            def evac(t):
                dve.wait_ge(turned, 2 * t + 1)
                for j in range(4):
                    ins = dve.tensor_scalar(h2[:, 0, j * P:(j + 1) * P], ps[:, 4 + 2 * (t % 2), j * P:(j + 1) * P],
                                            modT[:, 24 + j, 0:1], modT[:, 16 + j, 0:1], ALU.mult, ALU.add)
                ins.then_inc(ev_v, 1)
                dve.wait_ge(ev_v, t + 1)
                quads = lambda a: a.rearrange("p (j n) -> p j n", n=P)
                cols = slice(t * P, (t + 1) * P)
                step(dve.tensor_copy(hH[:, 0:4, cols], quads(h2[:, 0])))
                step(dve.tensor_tensor(hL[:, 0:4, cols], quads(h2[:, 0]), hH[:, 0:4, cols], ALU.subtract))
            dve.wait_ge(mod_mm, 1)
            step(dve.tensor_copy(modT[:, 16:32, 0], ps[:, 4, 0:2 * KD]))
            dve.wait_ge(mod_in[4], 16)
            gain = modT[:, 24:32, 0]
            step(dve.tensor_scalar(gain, gain, 1.0, None, ALU.add))
            step(dve.tensor_tensor(gain, gain, n2[:], ALU.mult))
            dve.sem_inc(mod_ok, 1)
            dve.wait_ge(g_in[0], 16)
            for t in range(LT):
                dve.wait_ge(mm, 2 * t + 2)
                step(dve.tensor_tensor(x1[:, t], ps[:, 2 * (t % 2):2 * (t % 2) + 2].rearrange("p b n -> p (b n)"), gate1[:], ALU.mult))
                dve.wait_ge(x_in[t % 2], 16 * (t // 2 + 1))
                dve.tensor_tensor(x1[:, t], x1[:, t], xt[:, t % 2], ALU.add).then_inc(x1_ok, 1)
                dve.wait_ge(rs_ok, t + 1)
                if t >= 2:
                    dve.wait_ge(turned, 2 * t - 2)
                dve.tensor_scalar(xn[:, t % 2], x1[:, t], ss[:, 2, t:t + 1], None, ALU.mult).then_inc(xn_ok, 1)
                if t >= 1:
                    evac(t - 1)
            evac(LT - 1)

        @block.scalar
        def _(act):
            step = Chain(act, chain_a)

            def evac(t):
                act.wait_ge(turned, 2 * t + 2)
                if t >= 1:
                    act.wait_ge(lo_ok, t)
                for j in range(4):
                    ins = act.activation(h2[:, 1, j * P:(j + 1) * P], ps[:, 5 + 2 * (t % 2), j * P:(j + 1) * P],
                                         ACT.Identity, bias=modT[:, 20 + j, 0:1], scale=modT[:, 28 + j, 0:1])
                ins.then_inc(ev_a, 1)
                act.wait_ge(ev_a, t + 1)
                act.activation(hH[:, 4:8, t * P:(t + 1) * P], h2[:, 1].rearrange("p (j n) -> p j n", n=P), ACT.Copy).then_inc(hi_ok, 1)
            act.wait_ge(mod_ok, 1)
            for t in range(LT):
                act.wait_ge(x1_ok, t + 1)
                if t >= 2:
                    act.wait_ge(turned, 2 * t - 2)
                step(act.activation(xn[:, t % 2], x1[:, t], ACT.Square, accum_out=ss[:, 0, t:t + 1]))
                step(act.activation(ss[:, 1, t:t + 1], ss[:, 0, t:t + 1], ACT.Ln, bias=eps[:], scale=1.0 / D))
                act.activation(ss[:, 2, t:t + 1], ss[:, 1, t:t + 1], ACT.Exp, scale=-0.5).then_inc(rs_ok, 1)
                if t >= 1:
                    evac(t - 1)
            evac(LT - 1)

        @block.gpsimd
        def _(pool):
            for t in range(LT):
                cols = slice(t * P, (t + 1) * P)
                pool.wait_ge(hi_ok, t + 1)
                pool.tensor_tensor(hL[:, 4:8, cols], h2[:, 1].rearrange("p (j n) -> p j n", n=P), hH[:, 4:8, cols],
                                   ALU.subtract).then_inc(lo_ok, 1)


WS = 512
SLICES = FF // WS
WT = WS // P
ITEMS = ((1, 0), (1, 1), (2, 0), (2, 1), (1, 2), (2, 2), (1, 3), (2, 3))


def mlp(k, keep, x1, hH, hL, gate2):
    nc, io = k.nc, k.io
    J1, J2, NI = 2 * WT, 2 * LT, len(ITEMS)
    with ExitStack() as st:
        sem = lambda n: k.sem(st, "f_" + n)
        raw = k.sb(st, "raw_w", [P, 2, D])
        w1 = [k.sb(st, n, [P, 2, D], F32R) for n in ("w1H", "w1L")]
        w2 = [k.sb(st, n, [P, WT, D], F32R) for n in ("w2H", "w2L")]
        hid = [k.sb(st, n, [P, WT, NLAT], F32R) for n in ("hidH", "hidL")]
        rl = k.sb(st, "rl", [P, 512])
        sq = k.sb(st, "sq_f", [P, 512])
        tmp = k.sb(st, "tmp_f", [P, 2, 512])
        ps = k.banks(st, "ps_f")
        raw_in = [sem(f"raw_in{j}") for j in range(2)]
        whi_ok, item_ok = sem("whi_ok"), sem("item_ok")
        mm1, relu_ok, sq_ok, hi_ok, hid_ok = (sem(n) for n in ("mm1", "relu_ok", "sq_ok", "hi_ok", "hid_ok"))
        mm2, gated, acc, out_ok = (sem(n) for n in ("mm2", "gated", "acc", "out_ok"))
        block = st.enter_context(nc.Block())
        v1 = io["w_mlp1"][0].rearrange("(k p) n -> p k n", p=P)
        v2 = io["w_mlp2"][0].rearrange("(k p) n -> p k n", p=P)
        h2 = (hH, hL)
        PARTS = ((0, 0), (1, 0), (0, 1))

        def item_at(w, j):
            return ITEMS.index((w, j)) + 1

        def over(eng, one_slice):
            with eng.Fori(0, SLICES - 1) as s:
                one_slice(s, True)
            one_slice(SLICES - 1, False)

        @block.sync
        def _(sp):
            def loads(s, first):
                for i, (w, j) in enumerate(ITEMS):
                    if not first:
                        sp.wait_ge(item_ok, NI * s + i - 1)
                    elif i >= 2:
                        sp.wait_ge(item_ok, i - 1)
                    dst = raw[:, i % 2]
                    if w == 1:
                        dst, src = dst.rearrange("p (k n) -> p k n", n=P), v1[:, :, bass.ds(s * WS + j * P, P)]
                    else:
                        src = v2[:, bass.ds(s * WT + j, 1)].rearrange("p a n -> p (a n)")
                    sp.dma_start(dst, src).then_inc(raw_in[i % 2], 16)
            loads(0, True)
            with sp.Fori(1, SLICES) as s:
                loads(s, False)
            for t in range(LT):
                sp.wait_ge(acc, PRIMED + J2 * (SLICES - 1) + 2 * t + 2)
                sp.dma_start(io["out"][0, t * P:(t + 1) * P], x1[:, t]).then_inc(out_ok, 16)
            sp.wait_ge(out_ok, 16 * LT)

        @block.tensor
        def _(pe):
            pe.sem_inc(mm1, PRIMED)
            pe.sem_inc(mm2, PRIMED)
            with pe.Fori(0, SLICES) as s:
                for n in range(J1):
                    j, half = n // 2, n % 2
                    if half == 0:
                        pe.wait_ge(item_ok, NI * s + item_at(1, j))
                    pe.wait_ge(relu_ok, PRIMED + J1 * s + max(n - 3, 0))
                    for kk in range(KD):
                        for a, b in PARTS:
                            ins = pe.matmul(ps[:, n % 4], w1[a][:, j % 2, kk * P:(kk + 1) * P], h2[b][:, kk, half * 512:half * 512 + 512],
                                            start=kk == 0 and (a, b) == PARTS[0], stop=kk == KD - 1 and (a, b) == PARTS[-1])
                    ins.then_inc(mm1, 1)
                for n in range(J2):
                    t, half = n // 2, n % 2
                    pe.wait_ge(gated, PRIMED + J2 * s + max(n - 3, 0))
                    if t == LT // 2 and half == 0:
                        pe.wait_ge(hid_ok, PRIMED + J1 * s + J1)
                    for kk in range(WT):
                        if n == 0:
                            pe.wait_ge(hid_ok, PRIMED + J1 * s + 2 * kk + 1)
                            pe.wait_ge(item_ok, NI * s + item_at(2, kk))
                        for a, b in PARTS:
                            ins = pe.matmul(ps[:, 4 + n % 4], hid[a][:, kk, t * P:(t + 1) * P], w2[b][:, kk, half * 512:half * 512 + 512],
                                            start=kk == 0 and (a, b) == PARTS[0], stop=kk == WT - 1 and (a, b) == PARTS[-1])
                    ins.then_inc(mm2, 1)

        @block.scalar
        def _(act):
            act.sem_inc(relu_ok, PRIMED)

            def item(s, w, j):
                i = ITEMS.index((w, j))
                act.wait_ge(raw_in[i % 2], 16 * (NI // 2 * s + i // 2 + 1))
                if w == 1:
                    act.wait_ge(mm1, PRIMED + J1 * s + 2 * (j - 2) + 2 if j >= 2 or not (isinstance(s, int) and s == 0) else PRIMED)
                    dst = w1[0][:, j % 2]
                else:
                    act.wait_ge(mm2, PRIMED + J2 * s)
                    dst = w2[0][:, j]
                act.activation(dst, raw[:, i % 2], ACT.Copy).then_inc(whi_ok, 1)

            def one_slice(s, more):
                def hidden(n):
                    act.wait_ge(mm1, PRIMED + J1 * s + n + 1)
                    act.activation(rl[:], ps[:, n % 4], ACT.Relu).then_inc(relu_ok, 1)
                    act.wait_ge(sq_ok, J1 * s + n + 1)
                    act.activation(hid[0][:, n // 2, (n % 2) * 512:(n % 2) * 512 + 512], sq[:], ACT.Copy).then_inc(hi_ok, 1)
                item(s, 2, 0)
                item(s, 2, 1)
                hidden(0)
                hidden(1)
                item(s, 1, 2)
                item(s, 2, 2)
                hidden(2)
                hidden(3)
                item(s, 1, 3)
                item(s, 2, 3)
                for n in range(4, J1):
                    hidden(n)
                if more:
                    item(s + 1, 1, 0)
                    item(s + 1, 1, 1)
            item(0, 1, 0)
            item(0, 1, 1)
            over(act, one_slice)

        @block.vector
        def _(dve):
            dve.sem_inc(gated, PRIMED)
            dve.sem_inc(hid_ok, PRIMED)

            def item(s, w, j):
                i = ITEMS.index((w, j))
                hi, lo = (w1[0][:, j % 2], w1[1][:, j % 2]) if w == 1 else (w2[0][:, j], w2[1][:, j])
                dve.wait_ge(whi_ok, NI * s + i + 1)
                dve.tensor_tensor(lo, raw[:, i % 2], hi, ALU.subtract).then_inc(item_ok, 1)

            def one_slice(s, more):
                def hidden(n):
                    dve.wait_ge(relu_ok, PRIMED + J1 * s + n + 1)
                    dve.wait_ge(hid_ok, PRIMED + J1 * s + n)
                    dve.tensor_tensor(sq[:], rl[:], rl[:], ALU.mult).then_inc(sq_ok, 1)
                    dve.wait_ge(hi_ok, J1 * s + n + 1)
                    at = (slice(None), n // 2, slice((n % 2) * 512, (n % 2) * 512 + 512))
                    dve.tensor_tensor(hid[1][at], sq[:], hid[0][at], ALU.subtract).then_inc(hid_ok, 1)
                item(s, 2, 0)
                item(s, 2, 1)
                hidden(0)
                hidden(1)
                item(s, 1, 2)
                item(s, 2, 2)
                hidden(2)
                hidden(3)
                item(s, 1, 3)
                item(s, 2, 3)
                for n in range(4, J1):
                    hidden(n)
                for n in range(J2):
                    dve.wait_ge(mm2, PRIMED + J2 * s + n + 1)
                    dve.wait_ge(acc, PRIMED + J2 * s + max(n - 1, 0))
                    dve.tensor_tensor(tmp[:, n % 2], ps[:, 4 + n % 4], gate2[:, (n % 2) * 512:(n % 2) * 512 + 512], ALU.mult).then_inc(gated, 1)
                    if more and n in (2, 5):
                        item(s + 1, 1, n // 3)
            item(0, 1, 0)
            item(0, 1, 1)
            over(dve, one_slice)

        @block.gpsimd
        def _(pool):
            pool.sem_inc(acc, PRIMED)
            with pool.Fori(0, SLICES) as s:
                for n in range(J2):
                    pool.wait_ge(gated, PRIMED + J2 * s + n + 1)
                    o = x1[:, n // 2, (n % 2) * 512:(n % 2) * 512 + 512]
                    pool.tensor_tensor(o, o, tmp[:, n % 2], ALU.add).then_inc(acc, 1)


def build(nc, io):
    k = Ctx(nc, io)
    with ExitStack() as root:
        keep = {"ident": k.sb(root, "ident", [P, P]), "masks": k.sb(root, "masks", [P, 4, P]),
                "modT": k.sb(root, "modT", [P, 32, 2]), "eps": k.sb(root, "eps", [P, 1]),
                "act_c": k.sb(root, "act_c", [P, KD, 2])}
        modulation(k, keep)
        with ExitStack() as st:
            hT = k.sb(st, "hT", [P, KD, NTOK])
            norm_in(k, keep, hT)
            ssd_tables(k, keep, hT)
        with ExitStack() as st:
            hH, hL = (k.sb(st, n, [P, KD, NTOK], F32R) for n in ("hTH", "hTL"))
            ssd_groups(k, keep, hH, hL)
        with ExitStack() as st:
            cqT = k.sb(st, "cqT", [P, 2, NLAT])
            ckvT = k.sb(st, "ckvT", [P, NTOK])
            kst = k.sb(st, "kst", [P, NT, 2, QKD])
            compress(k, keep, cqT, ckvT, kst)
            attention(k, keep, cqT, ckvT, kst)
        k.forget()
        merge(k, keep)
        with ExitStack() as st:
            x1 = k.sb(st, "x1", [P, LT, D])
            hH, hL = (k.sb(st, n, [P, KD, NLAT], F32R) for n in ("h2H", "h2L"))
            gate2 = k.sb(st, "gate2", [P, D])
            out_norm(k, keep, x1, hH, hL, gate2)
            mlp(k, keep, x1, hH, hL, gate2)


def _constants():
    a = np.arange(P)
    row, col = a[:, None], a[None, :]
    masks = np.stack([row <= col, row >= col, row < col, row > col], 1).astype(np.float32)
    pos = np.arange(NLAT)
    pairs = ROPE // 4
    freqs = np.float32(10000.0) ** (-np.arange(pairs, dtype=np.float32) / np.float32(pairs))
    ang = np.stack([pos // 64, pos % 64], -1).astype(np.float32)[..., None] * freqs
    cos, sin = np.cos(ang), np.sin(ang)
    cos2 = np.stack([cos, cos], 2).reshape(LT, P, ROPE)
    sin2 = np.stack([-sin, sin], 2).reshape(LT, P, ROPE)
    rope = np.stack([cos2, sin2], 0).transpose(2, 0, 1, 3)
    return {"ident": np.eye(P, dtype=np.float32), "masks": masks, "rope": np.ascontiguousarray(rope, np.float32)}


def _layouts(x):
    def cols(a):
        return a.reshape(-1, P).T
    cw = x["conv_w"][0].T.reshape(4 * GROUPS, P, TAPS)
    cb = x["conv_b"][0].reshape(4 * GROUPS, P, 1)
    conv = np.concatenate([cw, cb], -1)
    tiles = np.stack([np.stack([conv[2 * g], conv[2 * g + 1], conv[16 + g], conv[24 + g]], 0) for g in range(GROUPS)], 0)
    late = [3, 4, 2, 5]
    wm, bm = x["w_mod"][0].reshape(D, 6, D), x["b_mod"][0].reshape(6, D)
    return {
        "w_mod_late": np.concatenate([wm[:, i] for i in late], -1), "b_mod_late": np.concatenate([bm[i] for i in late], -1),
        "cvec": np.stack([cols(x["c"][0]), cols(x["c_ctx"])], -1),
        "b_modT": cols(x["b_mod"][0]), "norm1": cols(x["norm1_g"][0]), "norm2": cols(x["norm2_g"][0]),
        "q_gain": cols(x["q_a_g"][0]), "kv_gain": cols(x["kv_a_g"][0]),
        "conv": tiles.transpose(2, 0, 1, 3),
        "ssm_gain": x["ssm_norm_g"][0].reshape(GROUPS, 2, P).transpose(2, 0, 1),
        "w_late": np.concatenate([x["w_out"][0], x["w_proj_a"][0], x["w_proj_b"][0]], 0),
        "qk_gain": np.stack([x["qk_q_g"][0], x["qk_k_g"][0]], -1),
    }


_RAW = ["x", "ctx", "w_mod", "w_in", "w_uq", "w_ukv", "qk_q_g", "qk_k_g", "dt_bias", "a_log", "d_skip",
        "w_mlp1", "w_mlp2"]


def program(inputs, nc):
    x = {n: np.asarray(a) for n, a in inputs.items()}
    given = {n: x[n] for n in _RAW} | _layouts(x) | _constants()
    arrays, io = {}, {}
    for name, a in given.items():
        arrays[f"in_{name}"] = np.ascontiguousarray(a)
        io[name] = nc.dram_tensor(f"in_{name}", a.shape, F32, kind="ExternalInput").ap()
    io["out"] = nc.dram_tensor("out_0", (1, NLAT, D), F32, kind="ExternalOutput").ap()
    io["mod_rows"] = nc.dram_tensor("mod_rows", (KD, P, 512), F32, kind="Internal").ap()
    io["uT"] = nc.dram_tensor("uT_rows", (2 * GROUPS, P, NLAT), F32, kind="Internal").ap()
    io["hT"] = nc.dram_tensor("hT_rows", (KD, P, NTOK), F32, kind="Internal").ap()
    io["tab"] = nc.dram_tensor("tab_rows", (P, GROUPS, T_ALL), F32, kind="Internal").ap()
    mid = nc.dram_tensor("mid_rows", (PAIRS + KD, P, NLAT), F32, kind="Internal").ap()
    io["attT"], io["mT"] = mid[0:PAIRS], mid[PAIRS:]
    return arrays, io


def kernel(**inputs):
    import concourse.bacc as _bacc
    from concourse.bass_utils import run_bass_kernel_spmd as _run

    nc = _bacc.Bacc("TRN2", target_bir_lowering=False, num_devices=1)
    arrays, io = program(inputs, nc)
    build(nc, io)
    r = _run(nc, [arrays], core_ids=[0])
    return r.results[0]["out_0"]
```
